# Optimizing a Trainium2 kernel written in Bass

```python
import jax, jax.numpy as jnp
from jax import lax
import numpy as np

D_MODEL = 1024
BATCH = 1
SEQ = 512
DEPTH = 2

CHUNK = 64
N_MIXERS = 3
EPS = 1e-6
D_FF = 2816
N_NORMS = 6

A_HEADS = 8
A_DV = D_MODEL // A_HEADS
A_DQK = A_DV // 2
A_QK = A_HEADS * A_DQK
A_V = D_MODEL
A_CONV = 4
GATE_CAP = 15.0
A_IN = 2 * A_QK + 2 * A_V + 2 * A_HEADS

B_HEAD_DIM = 64
B_Q_HEADS = D_MODEL // B_HEAD_DIM
B_KV_HEADS = B_Q_HEADS // 8
B_GROUP = B_Q_HEADS // B_KV_HEADS
B_WINDOW = 128
B_WIN_CHUNKS = B_WINDOW // CHUNK
B_IN = (B_Q_HEADS + 2 * B_KV_HEADS) * B_HEAD_DIM

C_POOL = (2, 4, 8, 16)
C_GROUPS = len(C_POOL)
C_GC = D_MODEL // C_GROUPS

kernel_name = "hybrid_mlstm_swa_pool_macaron"

def _n_layers_of(kind):
    return (DEPTH - kind + N_MIXERS - 1) // N_MIXERS

def rmsnorm(x, g):
    x32 = x.astype(jnp.float32)
    y = x32 * lax.rsqrt(jnp.mean(x32 * x32, axis=-1, keepdims=True) + EPS)
    return (y * g.astype(jnp.float32)).astype(x.dtype)

def swiglu(h, w_gate, w_up, w_down):
    return (jax.nn.silu(h @ w_gate) * (h @ w_up)) @ w_down

def causal_conv(u, w, b):
    k_w = w.shape[0]
    s = u.shape[1]
    up = jnp.pad(u, ((0, 0), (k_w - 1, 0), (0, 0)))
    return b + sum(w[j] * up[:, j:j + s] for j in range(k_w))

def mlstm_mixer(h, w_in, conv_w, conv_b, gate_b, head_g, w_out):
    bsz, s, _ = h.shape
    nc = s // CHUNK
    proj = h @ w_in
    qk, v, o, g = jnp.split(proj, [2 * A_QK, 2 * A_QK + A_V, 2 * A_QK + 2 * A_V], axis=-1)
    qk = jax.nn.silu(causal_conv(qk, conv_w, conv_b)).astype(jnp.float32)
    q, k = jnp.split(qk, 2, axis=-1)
    k = k * (A_DQK ** -0.5)
    g = g.astype(jnp.float32) + gate_b.astype(jnp.float32)
    g = GATE_CAP * jnp.tanh(g / GATE_CAP)
    i_pre, f_pre = jnp.split(g, 2, axis=-1)
    log_f = jax.nn.log_sigmoid(f_pre)

    def to_chunks(t, d):
        return t.reshape(bsz, nc, CHUNK, A_HEADS, d).transpose(1, 0, 3, 2, 4)

    qc = to_chunks(q, A_DQK)
    kc = to_chunks(k, A_DQK)
    vc = to_chunks(v.astype(jnp.float32), A_DV)
    ic = i_pre.reshape(bsz, nc, CHUNK, A_HEADS).transpose(1, 0, 3, 2)
    bc = jnp.cumsum(log_f.reshape(bsz, nc, CHUNK, A_HEADS).transpose(1, 0, 3, 2), axis=-1)
    tril = jnp.tril(jnp.ones((CHUNK, CHUNK), dtype=bool))

    def step(carry, xs):
        c_st, n_st, m_st = carry
        q_, k_, v_, i_, b_ = xs
        log_d = b_[..., :, None] - b_[..., None, :] + i_[..., None, :]
        log_d = jnp.where(tril, log_d, -jnp.inf)
        prev = b_ + m_st[..., None]
        m_t = jnp.maximum(prev, jnp.max(log_d, axis=-1))
        dmat = jnp.exp(log_d - m_t[..., None])
        inter = jnp.exp(prev - m_t)
        sc = jnp.einsum('bhtd,bhsd->bhts', q_, k_) * dmat
        num = inter[..., None] * jnp.einsum('bhtd,bhde->bhte', q_, c_st) + jnp.einsum('bhts,bhse->bhte', sc, v_)
        den = inter * jnp.einsum('bhtd,bhd->bht', q_, n_st) + jnp.sum(sc, axis=-1)
        out = num / jnp.maximum(jnp.abs(den), jnp.exp(-m_t))[..., None]
        m_new = m_t[..., -1]
        w_st = jnp.exp(b_[..., -1:] - b_ + i_ - m_new[..., None])
        decay = jnp.exp(b_[..., -1] + m_st - m_new)
        c_new = decay[..., None, None] * c_st + jnp.einsum('bhs,bhsd,bhse->bhde', w_st, k_, v_)
        n_new = decay[..., None] * n_st + jnp.einsum('bhs,bhsd->bhd', w_st, k_)
        return (c_new, n_new, m_new), out

    init = (jnp.zeros((bsz, A_HEADS, A_DQK, A_DV), jnp.float32),
            jnp.zeros((bsz, A_HEADS, A_DQK), jnp.float32),
            jnp.zeros((bsz, A_HEADS), jnp.float32))
    _, hs = lax.scan(step, init, (qc, kc, vc, ic, bc))
    hs = hs.transpose(1, 0, 3, 2, 4)
    hs = hs * lax.rsqrt(jnp.mean(hs * hs, axis=-1, keepdims=True) + EPS)
    hs = hs.reshape(bsz, s, A_V) * head_g.astype(jnp.float32)
    hs = hs * jax.nn.sigmoid(o.astype(jnp.float32))
    return hs.astype(h.dtype) @ w_out

def _window_blocks(t):
    nc = t.shape[1]
    parts = [jnp.pad(t, ((0, 0), (j, 0), (0, 0), (0, 0), (0, 0)))[:, :nc]
             for j in range(B_WIN_CHUNKS - 1, -1, -1)]
    return jnp.concatenate(parts, axis=2)

def swa_mixer(h, w_in, sinks, w_out):
    bsz, s, _ = h.shape
    nc = s // CHUNK
    proj = h @ w_in
    q, k, v = jnp.split(proj, [B_Q_HEADS * B_HEAD_DIM, (B_Q_HEADS + B_KV_HEADS) * B_HEAD_DIM], axis=-1)
    q = q.reshape(bsz, nc, CHUNK, B_KV_HEADS, B_GROUP, B_HEAD_DIM)
    k_win = _window_blocks(k.reshape(bsz, nc, CHUNK, B_KV_HEADS, B_HEAD_DIM))
    v_win = _window_blocks(v.reshape(bsz, nc, CHUNK, B_KV_HEADS, B_HEAD_DIM))
    scores = jnp.einsum('bnqkgd,bnskd->bnkgqs', q, k_win).astype(jnp.float32) * (B_HEAD_DIM ** -0.5)
    back = jnp.repeat(jnp.arange(B_WIN_CHUNKS - 1, -1, -1), CHUNK)
    valid = jnp.arange(nc)[:, None] >= back[None, :]
    scores = jnp.where(valid[None, :, None, None, None, :], scores, -jnp.inf)
    sink = sinks.astype(jnp.float32).reshape(B_KV_HEADS, B_GROUP)[None, None, :, :, None, None]
    sink = jnp.broadcast_to(sink, scores.shape[:-1] + (1,))
    p = jax.nn.softmax(jnp.concatenate([scores, sink], axis=-1), axis=-1)[..., :-1]
    out = jnp.einsum('bnkgqs,bnskd->bnqkgd', p.astype(v_win.dtype), v_win)
    return out.reshape(bsz, s, D_MODEL) @ w_out

def pool_mixer(h, w_group, scale):
    bsz, s, _ = h.shape
    hf = h.astype(jnp.float32)
    cs = jnp.pad(jnp.cumsum(hf, axis=1), ((0, 0), (1, 0), (0, 0)))
    t = jnp.arange(s, dtype=jnp.float32)
    groups = []
    for gi, w in enumerate(C_POOL):
        csg = cs[..., gi * C_GC:(gi + 1) * C_GC]
        win_sum = csg[:, 1:] - jnp.pad(csg, ((0, 0), (w - 1, 0), (0, 0)))[:, :s]
        count = jnp.minimum(t + 1.0, float(w))[None, :, None]
        groups.append(win_sum / count - hf[..., gi * C_GC:(gi + 1) * C_GC])
    y = jnp.stack(groups, axis=2)
    y = jnp.einsum('bsgc,gcd->bsgd', y, w_group.astype(jnp.float32)).reshape(bsz, s, D_MODEL)
    return (y * scale.astype(jnp.float32)).astype(h.dtype)

def setup_inputs(seed: int = 0) -> dict:
    key = jax.random.key(seed)
    ks = jax.random.split(key, 20)
    n_a, n_b, n_c = _n_layers_of(0), _n_layers_of(1), _n_layers_of(2)

    def nrm(k, shape, fan_in):
        return jax.random.normal(k, shape, jnp.float32) * (fan_in ** -0.5)

    def gain(k, shape):
        return 1.0 + 0.02 * jax.random.normal(k, shape, jnp.float32)

    f_bias = jnp.linspace(3.0, 6.0, A_HEADS, dtype=jnp.float32)[None, :] + 0.1 * jax.random.normal(ks[9], (n_a, A_HEADS), jnp.float32)
    i_bias = 0.1 * jax.random.normal(ks[8], (n_a, A_HEADS), jnp.float32)
    return {
        "x": jax.random.normal(ks[0], (BATCH, SEQ, D_MODEL), jnp.float32),
        "norm_g": gain(ks[1], (DEPTH, N_NORMS, D_MODEL)),
        "ffn_w_gate": nrm(ks[2], (DEPTH, 2, D_MODEL, D_FF), D_MODEL),
        "ffn_w_up": nrm(ks[3], (DEPTH, 2, D_MODEL, D_FF), D_MODEL),
        "ffn_w_down": nrm(ks[4], (DEPTH, 2, D_FF, D_MODEL), D_FF),
        "a_w_in": nrm(ks[5], (n_a, D_MODEL, A_IN), D_MODEL),
        "a_conv_w": nrm(ks[6], (n_a, A_CONV, 2 * A_QK), A_CONV),
        "a_conv_b": 0.02 * jax.random.normal(ks[7], (n_a, 2 * A_QK), jnp.float32),
        "a_gate_b": jnp.concatenate([i_bias, f_bias], axis=-1),
        "a_head_g": gain(ks[10], (n_a, A_V)),
        "a_w_out": nrm(ks[11], (n_a, A_V, D_MODEL), A_V),
        "b_w_in": nrm(ks[12], (n_b, D_MODEL, B_IN), D_MODEL),
        "b_sinks": 0.5 * jax.random.normal(ks[13], (n_b, B_Q_HEADS), jnp.float32),
        "b_w_out": nrm(ks[14], (n_b, D_MODEL, D_MODEL), D_MODEL),
        "c_w_group": nrm(ks[15], (n_c, C_GROUPS, C_GC, C_GC), C_GC),
        "c_scale": gain(ks[16], (n_c, D_MODEL)),
    }

def reference(x, norm_g, ffn_w_gate, ffn_w_up, ffn_w_down, a_w_in, a_conv_w, a_conv_b,
              a_gate_b, a_head_g, a_w_out, b_w_in, b_sinks, b_w_out, c_w_group, c_scale):
    for i in range(DEPTH):
        g = norm_g[i]
        kind, j = i % N_MIXERS, i // N_MIXERS
        f1 = swiglu(rmsnorm(x, g[0]), ffn_w_gate[i, 0], ffn_w_up[i, 0], ffn_w_down[i, 0])
        x = x + 0.5 * rmsnorm(f1, g[1])
        hm = rmsnorm(x, g[2])
        if kind == 0:
            y = mlstm_mixer(hm, a_w_in[j], a_conv_w[j], a_conv_b[j], a_gate_b[j], a_head_g[j], a_w_out[j])
        elif kind == 1:
            y = swa_mixer(hm, b_w_in[j], b_sinks[j], b_w_out[j])
        else:
            y = pool_mixer(hm, c_w_group[j], c_scale[j])
        x = x + rmsnorm(y, g[3])
        f2 = swiglu(rmsnorm(x, g[4]), ffn_w_gate[i, 1], ffn_w_up[i, 1], ffn_w_down[i, 1])
        x = x + 0.5 * rmsnorm(f2, g[5])
    return x


_drawn_inputs = setup_inputs


def setup_inputs(seed=0):
    import zlib

    import numpy as np

    out = dict(_drawn_inputs(seed))
    spreads = {}
    factors = {'a_conv_b': 2.94, 'a_head_g': 3.421, 'b_sinks': 8.0}
    for name, (base, spread) in spreads.items():
        noise = np.random.default_rng([zlib.crc32(name.encode()), seed]).standard_normal(out[name].shape)
        drawn = base * np.exp(spread * noise) if base else spread * noise
        out[name] = __import__('jax').numpy.asarray(drawn.astype(out[name].dtype))
    for name, factor in factors.items():
        out[name] = (out[name] * factor).astype(out[name].dtype)
    return out
```

```python
from contextlib import ExitStack

import concourse.bass as bass
from concourse import mybir

F32 = mybir.dt.float32
F32R = mybir.dt.float32r
ALU = mybir.AluOpType
ACT = mybir.ActivationFunctionType
AX_X = mybir.AxisListType.X

P = 128
T = 512
D = 1024
KT = D // P
TT = T // P
F = 2816
FT = F // P
EPS = 1e-6
CHUNK = 64
NCH = T // CHUNK
DEPTH = 2
NORMS = 6

HEADS = 8
DQK = 64
TAPS = 4
CAP = 15.0

KV = 2
HD = 64

RING = 4
UNIT = 1024
DOWN = (8, 8, 6)

STAGES = ("ffn", "mlstm", "ffn", "ffn", "window", "ffn")
FFN_UNITS = 2 * FT + 3 * KT
M_V0, M_GATE, M_QK, M_V1, M_O, M_OUT, M_UNITS = 0, 4, 5, 13, 17, 25, 33
W_Q, W_K, W_V, W_OUT, W_UNITS = 0, 8, 9, 10, 18
UNITS = {"ffn": FFN_UNITS, "mlstm": M_UNITS, "window": W_UNITS}
BASE = [sum(UNITS[k] for k in STAGES[:s]) for s in range(len(STAGES) + 1)]
FFN_OF = {0: 0, 2: 1, 3: 2, 5: 3}
SET_OF = {0: 0, 1: 1, 2: 3, 3: 4, 4: 5, 5: 7}
OUT_SET = {1: 2, 4: 6}

C_GAIN = 0
C_HEADG = C_GAIN + DEPTH * NORMS * KT
C_CONVW = C_HEADG + HEADS
C_CONVB = C_CONVW + KT * TAPS
C_GATEB = C_CONVB + KT
C_SINK = C_GATEB + 1
C_ALL = C_SINK + 8

STAT = 7


def gain_col(stage, post, k):
    layer, j = divmod(stage, 3)
    return C_GAIN + (layer * NORMS + 2 * j + post) * KT + k


def build(nc, x_t, consts_d, gate_up, down, mlstm_w, window_w, out_t):
    with ExitStack() as ctx:
        def sb(name, shape, dt=F32, to=ctx):
            return to.enter_context(nc.sbuf_tensor(name, shape, dt))

        def sem(name):
            return ctx.enter_context(nc.semaphore(name))

        x = sb("x", [P, KT, T])
        raw = sb("raw", [P, RING, UNIT])
        w_hi = sb("w_hi", [P, RING, UNIT], F32R)
        w_lo = sb("w_lo", [P, RING, UNIT], F32R)
        consts = sb("consts", [P, C_ALL])
        half_gain = sb("half_gain", [P, C_CONVW])
        gate_b15 = sb("gate_b15", [P, 1])
        ident = sb("ident", [P, P])
        ones = sb("ones", [P, P])
        inv_d = sb("inv_d", [P, 1])
        inv_dv = sb("inv_dv", [P, 1])
        zeros = sb("zeros", [HEADS, T])
        rs = sb("rs", [P, T])
        acc = sb("acc", [P, T])
        sq = sb("sq", [P, 2, T])
        ms = sb("ms", [P, 4 * HEADS])
        root = sb("root", [P, 4 * HEADS])
        rcol = sb("rcol", [P, 4 * HEADS])
        ta = sb("ta", [P, T])
        tb = sb("tb", [P, T])
        tc = sb("tc", [P, T])
        x_hi = sb("x_hi", [P, KT, T], F32R)
        with ExitStack() as own:
            x_lo = sb("x_lo", [P, KT, T], F32R, own)
        with ExitStack() as own:
            y_ffn = sb("y_ffn", [P, KT, T], F32, own)
        ctx.enter_context(nc.sbuf_tensor("x_lo_room", [P, KT, T], F32))
        with ExitStack() as own:
            h_hi = sb("h_hi", [P, FT, T], F32R, own)
            h_lo = sb("h_lo", [P, FT, T], F32R, own)
        CAUSAL = [T - P * st for st in range(TT)]
        OFF = [sum(CAUSAL[:st]) for st in range(TT)]
        with ExitStack() as own:
            m_q = sb("m_q", [P, KT // 2, T], F32, own)
            m_k = [sb(f"m_k{par}", [P, KT // 2, T], F32, own) for par in range(2)]
            m_o = sb("m_o", [P, KT, T], F32, own)
            m_v = sb("m_v", [P, TT, D], F32, own)
            m_e = sb("m_e", [P, 2, sum(CAUSAL)], F32, own)
            m_sc = sb("m_sc", [P, 2, sum(CAUSAL)], F32, own)
            m_floor = sb("m_floor", [P, 2, T], F32, own)
            m_hs = sb("m_hs", [P, 2, T], F32, own)
            m_max = sb("m_max", [P, 2, T], F32, own)
        with ExitStack() as own:
            y_mix = sb("y_mix", [P, KT, T], F32, own)
        with ExitStack() as own:
            b_q = sb("b_q", [P, KT // 2, NCH, 2, CHUNK], F32, own)
            b_k = [[sb(f"b_k{g}{par}", [P, T], F32, own) for par in range(2)] for g in range(KV)]
            b_v = sb("b_v", [P, NCH, P], F32, own)
            b_p = sb("b_p", [P, 2, 8, P], F32, own)
            b_pt = sb("b_pt", [P, 2, 8, P], F32, own)
        ctx.enter_context(nc.sbuf_tensor("region", [P, 2 * FT, T], F32))
        u_conv = sb("u_conv", [P, TAPS - 1 + T])
        acol = sb("acol", [P, TT * HEADS])
        mx = sb("mx", [P, 2, 8])
        nmx = sb("nmx", [P, 2, 8])
        smx = sb("smx", [P, 2, 8])
        esk = sb("esk", [P, 2, 8])
        sm = sb("sm", [P, 2, 8])
        den = sb("den", [P, 2, 8])
        rden = sb("rden", [P, 2, 8])

        ps = ctx.enter_context(nc.psum_tensor("ps", [P, 8, T], F32))

        consts_landed = sem("consts_landed")
        x_landed = [sem(f"x_landed{i}") for i in range(2)]
        raw_landed = [sem(f"raw_landed{r}") for r in range(RING)]
        out_sent = sem("out_sent")
        hi_split = sem("hi_split")
        lo_split = sem("lo_split")
        unit_used = sem("unit_used")
        zeroed = sem("zeroed")
        selected = sem("selected")
        scaled_consts = sem("scaled_consts")
        op_hi = sem("op_hi")
        op_lo = sem("op_lo")
        sq_ready = sem("sq_ready")
        acc_done = sem("acc_done")
        acc_cleared = sem("acc_cleared")
        stat_sum = sem("stat_sum")
        ms_ready = sem("ms_ready")
        root_ready = sem("root_ready")
        rcol_ready = sem("rcol_ready")
        bcast_ready = sem("bcast_ready")
        rs_ready = sem("rs_ready")
        y_ready = sem("y_ready")
        y_scaled = sem("y_scaled")
        x_new = sem("x_new")
        gate_scaled = sem("gate_scaled")
        up_scaled = sem("up_scaled")
        silu_ready = sem("silu_ready")
        hid_ready = sem("hid_ready")
        hid_hi = sem("hid_hi")
        hid_lo = sem("hid_lo")
        region_zero = sem("region_zero")
        vchain = sem("vchain")
        achain = sem("achain")
        v_kept = sem("v_kept")
        gate_z = sem("gate_z")
        gate_tanh = sem("gate_tanh")
        gate_l = sem("gate_l")
        gates_done = sem("gates_done")
        acol_sum = sem("acol_sum")
        acol_ready = sem("acol_ready")
        qk_read = sem("qk_read")
        conv_ready = sem("conv_ready")
        qk_silu = sem("qk_silu")
        k_placed = sem("k_placed")
        o_read = sem("o_read")
        o_tanh = sem("o_tanh")
        s_ready = sem("s_ready")
        maxes_ready = sem("maxes_ready")
        e_ready = sem("e_ready")
        e_masked = sem("e_masked")
        floor_ready = sem("floor_ready")
        sc_done = sem("sc_done")
        num_ready = sem("num_ready")
        den_ready = sem("den_ready")
        abs_ready = sem("abs_ready")
        hs_ready = sem("hs_ready")
        hsq_ready = sem("hsq_ready")
        stat_heads = sem("stat_heads")
        og_ready = sem("og_ready")
        head_bcast = sem("head_bcast")
        og_scaled = sem("og_scaled")
        b_read = sem("b_read")
        bv_ready = sem("bv_ready")
        bw_ready = sem("bw_ready")
        bw_kept = sem("bw_kept")
        bs_ready = sem("bs_ready")
        nmx_ready = sem("nmx_ready")
        smx_ready = sem("smx_ready")
        p_exp = sem("p_exp")
        p_ready = sem("p_ready")
        pt_ready = sem("pt_ready")
        pt_act = sem("pt_act")
        pt_dve = sem("pt_dve")
        po_ready = sem("po_ready")

        block = ctx.enter_context(nc.Block())

        @block.sync
        def _(sp):
            sp.dma_start(consts[:, :], consts_d).then_inc(consts_landed, 16)
            for i in range(2):
                half = slice(i * KT // 2, (i + 1) * KT // 2)
                sp.dma_start(x[:, half, :], x_t[:, half, :]).then_inc(x_landed[i], 16)

            def load(u, first, src):
                if not first:
                    sp.wait_ge(lo_split, u - RING + 1)
                slot = u_slot(u)
                sp.dma_start(raw[:, slot, 0:src.shape[-1]], src).then_inc(raw_landed[slot], 16)

            def u_slot(u):
                return slot_of[0]

            slot_of = [0]

            def load_unit(c, m, i, src):
                slot_of[0] = c % RING
                load(c + m * i, isinstance(i, int) and c + m * i < RING, src)

            for s, kind in enumerate(STAGES):
                ub = BASE[s]
                if kind == "ffn":
                    n = FFN_OF[s]
                    for u in range(4):
                        load_unit(ub + u, 0, 0, gate_up[n, u])
                    with sp.Fori(1, FT // 2) as i:
                        for u in range(4):
                            load_unit(ub + u, 4, i, gate_up[n, bass.ds(4 * i + u, 1)].rearrange("a p c -> (a p) c"))
                    with sp.Fori(0, KT // 4) as i:
                        for d in range(4):
                            tile = down[n, bass.ds(4 * i + d, 1)].rearrange("a p c -> (a p) c")
                            at = 0
                            for b, blocks in enumerate(DOWN):
                                load_unit(ub + 2 * FT + 3 * d + b, 12, i, tile[:, at:at + blocks * P])
                                at += blocks * P
                else:
                    src = mlstm_w if kind == "mlstm" else window_w
                    for u in range(UNITS[kind]):
                        load_unit(ub + u, 0, 0, src[u])
            last = len(STAGES) - 1
            for k in range(KT):
                sp.wait_ge(x_new, KT * last + k + 1)
                sp.dma_start(out_t[:, k, :], x[:, k, :]).then_inc(out_sent, 16)
            sp.wait_ge(out_sent, 16 * KT)

        @block.gpsimd
        def _(pool):
            pool.memset(ident[:, :], 0.0).then_inc(zeroed, 1)
            pool.wait_ge(zeroed, 1)
            pool.affine_select(out=ident[:, :], in_=ident[:, :], compare_op=ALU.not_equal, fill=1.0, base=0,
                               pattern=[[-1, P]], channel_multiplier=1).then_inc(selected, 1)
            pool.memset(ones[:, :], 1.0).then_inc(zeroed, 1)
            pool.memset(inv_d[:, :], 1.0 / D).then_inc(zeroed, 1)
            pool.memset(inv_dv[:, :], 1.0 / P).then_inc(zeroed, 1)
            pool.memset(zeros[:, :], 0.0).then_inc(zeroed, 1)
            pool.memset(u_conv[:, 0:TAPS - 1], 0.0).then_inc(zeroed, 1)

            pool.wait_ge(unit_used, BASE[1])
            pool.memset(m_k[0][HD:P, :, :], 0.0).then_inc(region_zero, 1)
            pool.wait_ge(region_zero, 1)
            pool.memset(m_k[1][0:HD, :, :], 0.0).then_inc(region_zero, 1)
            pool.wait_ge(region_zero, 2)
            pool.memset(m_max[:, :, :], 0.0).then_inc(region_zero, 1)
            for c in range(KT // 2):
                pool.wait_ge(qk_silu, KT // 2 + c + 1)
                for par in range(2):
                    rows = slice(par * HD, par * HD + HD)
                    pool.wait_ge(region_zero, 3)
                    if c + par:
                        pool.wait_ge(k_placed, 2 * c + par)
                    pool.tensor_scalar(m_k[par][rows, c, :], tc[rows, :], DQK ** -0.5, None,
                                       ALU.mult).then_inc(k_placed, 1)
            pool.wait_ge(k_placed, KT)
            for h in range(HEADS):
                for st in range(TT):
                    pool.wait_ge(e_ready, TT * h + st + 1)
                    diag = m_e[:, h % 2, OFF[st]:OFF[st] + P]
                    pool.affine_select(out=diag, in_=diag, compare_op=ALU.is_ge, fill=0.0, base=0,
                                       pattern=[[1, P]], channel_multiplier=-1).then_inc(e_masked, 1)

            pool.wait_ge(unit_used, BASE[4])
            for g in range(KV):
                pool.wait_ge(region_zero, 3 + 2 * g)
                pool.memset(b_k[g][0][HD:P, :], 0.0).then_inc(region_zero, 1)
                pool.wait_ge(region_zero, 3 + 2 * g + 1)
                pool.memset(b_k[g][1][0:HD, :], 0.0).then_inc(region_zero, 1)

        @block.scalar
        def _(act):
            steps = [0]

            def link(ins):
                steps[0] += 1
                ins.then_inc(achain, 1)
                act.wait_ge(achain, steps[0])

            def split_hi(c, m=0, i=0, cols=UNIT):
                slot, u = c % RING, c + m * i
                act.wait_ge(raw_landed[slot], 16 * (c // RING + 1) + 16 * (m // RING) * i)
                if c >= RING:
                    act.wait_ge(unit_used, u - RING + 1)
                act.activation(w_hi[:, slot, 0:cols], raw[:, slot, 0:cols], ACT.Copy).then_inc(hi_split, 1)

            def square(q, m, i, src):
                if q >= 2:
                    act.wait_ge(acc_done, q - 1 + m * i)
                act.activation(sq[:, q % 2, :], src, ACT.Square).then_inc(sq_ready, 1)

            def input_tiles(s):
                for k in range(KT):
                    if s == 0:
                        act.wait_ge(x_landed[k // (KT // 2)], 16)
                        if k == 0:
                            act.wait_ge(consts_landed, 16)
                    else:
                        act.wait_ge(x_new, KT * (s - 1) + k + 1)
                    g = gain_col(s, 0, k)
                    act.activation(x_hi[:, k, :], x[:, k, :], ACT.Copy, scale=consts[:, g:g + 1]).then_inc(op_hi, 1)
                    square(16 * s + k, 0, 0, x[:, k, :])

            def sqrt_stat(n, cols=TT):
                act.wait_ge(ms_ready, n + 1)
                act.activation(root[:, 0:cols], ms[:, 0:cols], ACT.Sqrt).then_inc(root_ready, 1)

            def keep_rs(s):
                act.wait_ge(bcast_ready, 2 * s + 1)
                act.activation(rs[:, :], ps[:, STAT, :], ACT.Copy).then_inc(rs_ready, 1)

            def output_tile(s, c, m, i, bank, gain, y, used):
                act.wait_ge(unit_used, used)
                d = c + m * i
                col = gain_col(s, 1, 0) + d
                dst = y[:, bass.ds(d, 1), :].rearrange("p a t -> p (a t)")
                act.activation(dst, ps[:, bank, :], ACT.Copy, scale=gain[:, bass.ds(col, 1)]).then_inc(y_ready, 1)
                square(16 * s + 8 + c, m, i, ps[:, bank, :])

            def hidden(e, c, m, i):
                act.wait_ge(gate_scaled, e + m * i + 1)
                act.activation(tc[:, :], ta[:, :], ACT.Silu).then_inc(silu_ready, 1)
                act.wait_ge(hid_ready, e + m * i + 1)
                dst = h_hi[:, bass.ds(c + m * i, 1), :].rearrange("p a t -> p (a t)")
                act.activation(dst, tb[:, :], ACT.Copy).then_inc(hid_hi, 1)

            def ffn(s):
                ub, e0 = BASE[s], FT * FFN_OF[s]
                input_tiles(s)
                split_hi(ub + 3)
                sqrt_stat(stat_no(s, 0))
                split_hi(ub + 4)
                keep_rs(s)
                split_hi(ub + 5)
                hidden(e0, 0, 0, 0)
                hidden(e0 + 1, 1, 0, 0)
                with act.Fori(1, FT // 2) as i:
                    for j in range(2):
                        split_hi(ub + 2 * j + 2, 4, i)
                        split_hi(ub + 2 * j + 3, 4, i)
                        hidden(e0 + j, j, 2, i)
                vb = ub + 2 * FT

                def four_tiles(i, splits=12):
                    for d in range(4):
                        for b in range(3):
                            if 3 * d + b < splits:
                                split_hi(vb + 3 * d + b + 2, 12, i, DOWN[(b + 2) % 3] * P)
                        output_tile(s, d, 4, i, 4 + d % 2, half_gain, y_ffn, vb + 3 * d + 3 + 12 * i)

                last = s + 1 == len(STAGES)
                with act.Fori(0, KT // 4 - last) as i:
                    four_tiles(i)
                if last:
                    four_tiles(KT // 4 - 1, 10)
                post(s)

            def post(s):
                if s + 1 < len(STAGES):
                    split_hi(BASE[s + 1] + 2)
                sqrt_stat(stat_no(s, 1))

            def mlstm(s):
                ub = BASE[s]
                input_tiles(s)
                for u in range(M_UNITS):
                    if u == M_GATE:
                        sqrt_stat(stat_no(s, 0))
                        keep_rs(s)
                        keep_v(0)
                    if 1 <= u and u != M_OUT:
                        split_hi(ub + u + 2)
                    if u == M_GATE:
                        act.wait_ge(gate_z, 1)
                        act.activation(tc[0:40, :], ta[0:40, :], ACT.Tanh, bias=gate_b15[0:40, :],
                                       scale=1.0 / CAP).then_inc(gate_tanh, 1)
                        act.wait_ge(gate_tanh, 1)
                        link(act.activation(tb[0:HEADS, :], tc[32:40, :], ACT.Exp, scale=-CAP))
                        act.activation(m_e[0:HEADS, 0, T:2 * T], tb[0:HEADS, :], ACT.Ln,
                                       bias=ones[0:HEADS, 0:1]).then_inc(gate_l, 1)
                    if M_QK <= u < M_QK + KT:
                        c = u - M_QK
                        act.wait_ge(conv_ready, c + 1)
                        src = (ta, tb)[c % 2]
                        if c < KT // 2:
                            dst = m_q[:, c, :]
                        else:
                            dst = tc[:, :]
                            if c > KT // 2:
                                act.wait_ge(k_placed, 2 * (c - KT // 2))
                        act.activation(dst, src[:, :], ACT.Silu).then_inc(qk_silu, 1)
                    if u == M_V1 + 3:
                        keep_v(1)
                    if M_O <= u < M_O + KT:
                        c = u - M_O
                        act.wait_ge(o_read, c + 1)
                        act.activation(m_o[:, c, :], (ta, tb)[c % 2][:, :], ACT.Tanh, scale=0.5).then_inc(o_tanh, 1)
                    if u == M_OUT - 1:
                        split_hi(ub + M_OUT + 2)
                        heads(s)
                    if M_OUT <= u:
                        d = u - M_OUT
                        output_tile(s, d, 0, 0, 4 + d % 3, consts, y_mix, used_out(s, d))
                post(s)

            def keep_v(half):
                act.wait_ge(unit_used, BASE[1] + (M_V0 if half == 0 else M_V1) + 4)
                act.wait_ge(rcol_ready, stat_no(1, 0) + 1)
                for tt in range(TT):
                    act.activation(m_v[:, tt, half * T:half * T + T], ps[:, tt, :], ACT.Copy,
                                   scale=rcol[:, tt:tt + 1]).then_inc(v_kept, 1)

            def heads(s):
                act.wait_ge(acol_ready, 1)
                for h in range(HEADS + 1):
                    if h < HEADS:
                        act.wait_ge(maxes_ready, h + 1)
                        if h >= 2:
                            act.wait_ge(sc_done, TT * (h - 1))
                        for st in range(TT):
                            act.activation(m_e[:, h % 2, OFF[st]:OFF[st] + CAUSAL[st]], ps[:, 3, P * st:T], ACT.Exp,
                                           bias=acol[:, st * HEADS + h:st * HEADS + h + 1]).then_inc(e_ready, 1)
                        if h >= 2:
                            act.wait_ge(hs_ready, h - 1)
                        act.activation(m_floor[:, h % 2, :], ps[:, 4, :], ACT.Exp).then_inc(floor_ready, 1)
                    if h >= 1:
                        if h >= 2:
                            act.wait_ge(hs_ready, h - 1)
                        act.wait_ge(den_ready, h)
                        act.activation(ta[:, :], ps[:, 6, :], ACT.Abs).then_inc(abs_ready, 1)
                        act.wait_ge(hs_ready, h)
                        if h >= 3:
                            act.wait_ge(stat_heads, h - 2)
                        act.activation(sq[:, h % 2, :], m_hs[:, (h - 1) % 2, :], ACT.Square).then_inc(hsq_ready, 1)
                sqrt_stat(stat_no(1, 0) + 1, 4 * HEADS)
                for h in range(HEADS):
                    act.wait_ge(og_scaled, h + 1)
                    act.activation(x_hi[:, h, :], m_o[:, h, :], ACT.Copy,
                                   scale=half_gain[:, C_HEADG + h:C_HEADG + h + 1]).then_inc(op_hi, 1)

            def window(s):
                ub = BASE[s]
                input_tiles(s)
                split_hi(ub + 3)
                sqrt_stat(stat_no(s, 0))
                split_hi(ub + 4)
                keep_rs(s)
                split_hi(ub + 5)
                for u in range(W_UNITS):
                    if 4 <= u and u != W_OUT:
                        split_hi(ub + u + 2)
                    if u == W_V:
                        split_hi(ub + W_OUT + 2)
                        act.wait_ge(bw_ready, 8)
                        act.activation(b_v[0:CHUNK, 0, :], ps[0:CHUNK, 4, 0:P], ACT.Copy).then_inc(bw_kept, 1)
                        act.activation(b_v[:, 1:4, :], ps[:, 4, P:T].rearrange("p (a b) -> p a b", a=3),
                                       ACT.Copy).then_inc(bw_kept, 1)
                        act.activation(b_v[:, 4:8, :], ps[:, 5, :].rearrange("p (a b) -> p a b", a=4),
                                       ACT.Copy).then_inc(bw_kept, 1)
                        for n in range(NCH + 1):
                            if n < NCH:
                                chunk_exp(n)
                            if n >= 1:
                                chunk_out(n - 1)
                    if W_OUT <= u:
                        d = u - W_OUT
                        output_tile(s, d, 0, 0, 4 + d % 3, consts, y_mix, used_out(s, d))
                post(s)

            def chunk_exp(n):
                keys = slice(0, CHUNK if n == 0 else P)
                act.wait_ge(nmx_ready, n + 1)
                if n >= 2:
                    act.wait_ge(pt_ready, n - 1)
                for i in range(8):
                    act.activation(b_p[:, n % 2, i, keys], ps[:, 2 * (n % 2) + i // 4, :].rearrange(
                        "p (a b) -> p a b", a=4)[:, i % 4, keys], ACT.Exp, bias=nmx[:, n % 2, i:i + 1],
                        accum_out=sm[:, n % 2, i:i + 1]).then_inc(p_exp, 1)
                act.wait_ge(smx_ready, n + 1)
                act.activation(esk[:, n % 2, :], smx[:, n % 2, :], ACT.Exp).then_inc(p_exp, 1)

            def chunk_out(n):
                rows = slice(0, CHUNK if n == 0 else P)
                act.wait_ge(pt_ready, n + 1)
                if n >= 2:
                    act.wait_ge(po_ready, n - 1)
                act.activation(b_pt[rows, n % 2, 0:4, :], ps[rows, 4, :].rearrange("p (a b) -> p a b", a=4),
                               ACT.Copy).then_inc(pt_act, 1)
                act.wait_ge(po_ready, n + 1)
                act.activation(x_hi[:, :, n * CHUNK:(n + 1) * CHUNK],
                               ps[:, 6 + n % 2, :].rearrange("p (a b) -> p a b", a=8), ACT.Copy).then_inc(op_hi, 1)

            for u in range(3):
                split_hi(u)
            for s, kind in enumerate(STAGES):
                {"ffn": ffn, "mlstm": mlstm, "window": window}[kind](s)

        @block.vector
        def _(dve):
            steps = [0]

            def link(ins):
                steps[0] += 1
                ins.then_inc(vchain, 1)
                dve.wait_ge(vchain, steps[0])

            def split_lo(c, m=0, i=0, cols=UNIT):
                slot, u = c % RING, c + m * i
                dve.wait_ge(hi_split, u + 1)
                dve.tensor_tensor(w_lo[:, slot, 0:cols], raw[:, slot, 0:cols], w_hi[:, slot, 0:cols].bitcast(F32),
                                  ALU.subtract).then_inc(lo_split, 1)

            def add_square(q, m, i, n):
                dve.wait_ge(acc_cleared, n + 1)
                if q >= 1:
                    dve.wait_ge(acc_done, q + m * i)
                dve.wait_ge(sq_ready, q + m * i + 1)
                dve.tensor_tensor(acc[:, :], acc[:, :], sq[:, q % 2, :], ALU.add).then_inc(acc_done, 1)

            def input_lo(s, k):
                g = gain_col(s, 0, k)
                dve.wait_ge(op_hi, KT * SET_OF[s] + k + 1)
                dve.scalar_tensor_tensor(out=x_lo[:, k, :], in0=x[:, k, :], scalar=consts[:, g:g + 1],
                                         in1=x_hi[:, k, :].bitcast(F32), op0=ALU.mult,
                                         op1=ALU.subtract).then_inc(op_lo, 1)
                add_square(16 * s + k, 0, 0, 2 * s)

            def residual(s, k, y):
                dve.wait_ge(bcast_ready, 2 * s + 2)
                dve.wait_ge(y_ready, KT * s + k + 1)
                dve.tensor_tensor(y[:, k, :], y[:, k, :], ps[:, STAT, :], ALU.mult).then_inc(y_scaled, 1)
                dve.wait_ge(y_scaled, KT * s + k + 1)
                dve.tensor_tensor(x[:, k, :], x[:, k, :], y[:, k, :], ALU.add).then_inc(x_new, 1)

            def input_tiles(s):
                y = y_of(s - 1)
                for k in range(KT + 1):
                    if s and k < KT:
                        residual(s - 1, k, y)
                    if k >= 1:
                        input_lo(s, k - 1)

            def y_of(s):
                return y_ffn if s >= 0 and STAGES[s] == "ffn" else y_mix

            def stat_ms(n, cols=TT, clear=True):
                dve.wait_ge(stat_sum, n + 1)
                dve.tensor_scalar(ms[:, 0:cols], ps[:, STAT, 0:cols], EPS, None, ALU.add).then_inc(ms_ready, 1)
                if clear:
                    dve.memset(acc[:, :], 0.0).then_inc(acc_cleared, 1)

            def stat_rcol(n, cols=TT):
                dve.wait_ge(root_ready, n + 1)
                dve.reciprocal(rcol[:, 0:cols], root[:, 0:cols]).then_inc(rcol_ready, 1)

            def hidden(e, ub, c, m, i):
                n = e + m * i
                dve.wait_ge(unit_used, ub + 2 * c + 1 + 2 * m * i)
                dve.tensor_tensor(ta[:, :], ps[:, 2 * (c % 2), :], rs[:, :], ALU.mult).then_inc(gate_scaled, 1)
                dve.wait_ge(unit_used, ub + 2 * c + 2 + 2 * m * i)
                if e or not isinstance(i, int):
                    dve.wait_ge(hid_lo, n)
                dve.tensor_tensor(tb[:, :], ps[:, 2 * (c % 2) + 1, :], rs[:, :], ALU.mult).then_inc(up_scaled, 1)
                dve.wait_ge(up_scaled, n + 1)
                dve.wait_ge(silu_ready, n + 1)
                dve.tensor_tensor(tb[:, :], tb[:, :], tc[:, :], ALU.mult).then_inc(hid_ready, 1)
                dve.wait_ge(hid_hi, n + 1)
                f = bass.ds(c + m * i, 1)
                dve.tensor_tensor(h_lo[:, f, :].rearrange("p a t -> p (a t)"), tb[:, :],
                                  h_hi[:, f, :].rearrange("p a t -> p (a t)").bitcast(F32),
                                  ALU.subtract).then_inc(hid_lo, 1)

            def ffn(s):
                ub, e0 = BASE[s], FT * FFN_OF[s]
                input_tiles(s)
                split_lo(ub + 3)
                stat_ms(stat_no(s, 0))
                split_lo(ub + 4)
                stat_rcol(stat_no(s, 0))
                split_lo(ub + 5)
                dve.wait_ge(rs_ready, s + 1)
                hidden(e0, ub, 0, 0, 0)
                hidden(e0 + 1, ub, 1, 0, 0)
                with dve.Fori(1, FT // 2) as i:
                    for j in range(2):
                        split_lo(ub + 2 * j + 2, 4, i)
                        split_lo(ub + 2 * j + 3, 4, i)
                        hidden(e0 + j, ub, j, 2, i)
                vb = ub + 2 * FT

                def four_tiles(i, splits=12):
                    for d in range(4):
                        for b in range(3):
                            if 3 * d + b < splits:
                                split_lo(vb + 3 * d + b + 2, 12, i, DOWN[(b + 2) % 3] * P)
                        add_square(16 * s + 8 + d, 4, i, 2 * s + 1)

                last = s + 1 == len(STAGES)
                with dve.Fori(0, KT // 4 - last) as i:
                    four_tiles(i)
                if last:
                    four_tiles(KT // 4 - 1, 10)
                post(s)

            def post(s):
                stat_ms(stat_no(s, 1))
                if s + 1 < len(STAGES):
                    split_lo(BASE[s + 1] + 2)
                stat_rcol(stat_no(s, 1))

            def mlstm(s):
                ub = BASE[s]
                input_tiles(s)
                for u in range(M_UNITS):
                    if u == M_GATE:
                        stat_ms(stat_no(s, 0))
                        stat_rcol(stat_no(s, 0))
                    if 1 <= u and u != M_OUT:
                        split_lo(ub + u + 2)
                    if u == M_GATE:
                        gates(ub)
                    if M_QK <= u < M_QK + KT:
                        qk_tile(ub, u, u - M_QK)
                    if u == M_V1 + 3:
                        dve.wait_ge(acol_sum, 1)
                        dve.tensor_copy(acol[:, :], ps[:, 6, 0:TT * HEADS]).then_inc(acol_ready, 1)
                    if M_O <= u < M_O + KT:
                        c = u - M_O
                        dve.wait_ge(unit_used, ub + u + 1)
                        if c >= 2:
                            dve.wait_ge(o_tanh, c - 1)
                        else:
                            dve.wait_ge(qk_silu, KT)
                        dve.tensor_tensor((ta, tb)[c % 2][:, :], ps[:, 4 + c % 2, :], rs[:, :],
                                          ALU.mult).then_inc(o_read, 1)
                    if u == M_OUT - 1:
                        split_lo(ub + M_OUT + 2)
                        heads(s)
                    if M_OUT <= u:
                        add_square(16 * s + 8 + u - M_OUT, 0, 0, 2 * s + 1)
                post(s)

            def gates(ub):
                dve.wait_ge(unit_used, ub + M_GATE + 1)
                dve.wait_ge(rs_ready, 2)
                dve.tensor_tensor(ta[0:40, :], ps[0:40, 6, :], rs[0:40, :], ALU.mult).then_inc(gate_z, 1)
                dve.wait_ge(gate_l, 1)
                run, soft = m_e[0:HEADS, 0, 0:T], m_e[0:HEADS, 0, T:2 * T]
                a, top = m_e[0:HEADS, 1, 0:T], m_e[0:HEADS, 1, T:2 * T]
                dve.wait_ge(zeroed, 6)
                link(dve.tensor_tensor_scan(run, zeros[:, :], soft, 0.0, ALU.add, ALU.add))
                link(dve.scalar_tensor_tensor(out=a, in0=tc[0:HEADS, :], scalar=CAP, in1=run, op0=ALU.mult,
                                              op1=ALU.add))
                link(dve.tensor_tensor_scan(top, zeros[:, :], a, 0.0, ALU.add, ALU.max))
                dve.wait_ge(region_zero, 3)
                dve.tensor_scalar(m_max[0:HEADS, 0, :], top, -1.0, None, ALU.mult).then_inc(gates_done, 1)
                dve.tensor_tensor(m_max[0:HEADS, 1, :], run, top, ALU.subtract).then_inc(gates_done, 1)

            def qk_tile(ub, u, c):
                dve.wait_ge(unit_used, ub + u + 1)
                dve.tensor_tensor(u_conv[:, TAPS - 1:], ps[:, 4 + c % 2, :], rs[:, :], ALU.mult).then_inc(qk_read, 1)
                dve.wait_ge(qk_read, c + 1)
                buf = (ta, tb)[c % 2][:, :]
                if c >= 2:
                    dve.wait_ge(qk_silu, c - 1)
                w = C_CONVW + c * TAPS
                for j in range(TAPS):
                    if j == 0:
                        ins = dve.tensor_scalar(buf, u_conv[:, 0:T], consts[:, w:w + 1],
                                                consts[:, C_CONVB + c:C_CONVB + c + 1], ALU.mult, ALU.add)
                    else:
                        ins = dve.scalar_tensor_tensor(out=buf, in0=u_conv[:, j:j + T],
                                                       scalar=consts[:, w + j:w + j + 1], in1=buf,
                                                       op0=ALU.mult, op1=ALU.add)
                    if j < TAPS - 1:
                        link(ins)
                    else:
                        ins.then_inc(conv_ready, 1)

            def heads(s):
                for h in range(HEADS + 1):
                    if h < HEADS:
                        dve.wait_ge(s_ready, h + 1)
                        if h >= 2:
                            dve.wait_ge(den_ready, h - 1)
                        for st in range(TT):
                            dve.wait_ge(e_masked, TT * h + st + 1)
                            bank, at = ((0, 0), (1, 0), (2, 0), (2, 256))[st]
                            dve.tensor_tensor(m_sc[:, h % 2, OFF[st]:OFF[st] + CAUSAL[st]],
                                              m_e[:, h % 2, OFF[st]:OFF[st] + CAUSAL[st]],
                                              ps[:, bank, at:at + CAUSAL[st]], ALU.mult).then_inc(sc_done, 1)
                    if h >= 1:
                        g = h - 1
                        dve.wait_ge(floor_ready, g + 1)
                        dve.wait_ge(abs_ready, g + 1)
                        link(dve.tensor_tensor(tb[:, :], ta[:, :], m_floor[:, g % 2, :], ALU.max))
                        link(dve.reciprocal(tb[:, :], tb[:, :]))
                        dve.wait_ge(num_ready, g + 1)
                        if g >= 2:
                            dve.wait_ge(hsq_ready, g - 1)
                        dve.tensor_tensor(m_hs[:, g % 2, :], tb[:, :], ps[:, 5, :], ALU.mult).then_inc(hs_ready, 1)
                        dve.wait_ge(hs_ready, g + 1)
                        dve.scalar_tensor_tensor(out=m_o[:, g, :], in0=m_o[:, g, :], scalar=1.0,
                                                 in1=m_hs[:, g % 2, :], op0=ALU.add,
                                                 op1=ALU.mult).then_inc(og_ready, 1)
                n = stat_no(1, 0) + 1
                stat_ms(n, 4 * HEADS, clear=False)
                stat_rcol(n, 4 * HEADS)
                for h in range(HEADS + 1):
                    if h < HEADS:
                        dve.wait_ge(head_bcast, h + 1)
                        dve.wait_ge(og_ready, h + 1)
                        dve.tensor_tensor(m_o[:, h, :], m_o[:, h, :], ps[:, (3, 7)[h % 2], :],
                                          ALU.mult).then_inc(og_scaled, 1)
                    if h >= 1:
                        g = h - 1
                        dve.wait_ge(op_hi, KT * OUT_SET[s] + g + 1)
                        dve.wait_ge(og_scaled, g + 1)
                        col = C_HEADG + g
                        dve.scalar_tensor_tensor(out=x_lo[:, g, :], in0=m_o[:, g, :],
                                                 scalar=half_gain[:, col:col + 1],
                                                 in1=x_hi[:, g, :].bitcast(F32), op0=ALU.mult,
                                                 op1=ALU.subtract).then_inc(op_lo, 1)

            def window(s):
                ub = BASE[s]
                input_tiles(s)
                split_lo(ub + 3)
                stat_ms(stat_no(s, 0))
                split_lo(ub + 4)
                stat_rcol(stat_no(s, 0))
                split_lo(ub + 5)
                dve.wait_ge(rs_ready, s + 1)
                for u in range(W_UNITS):
                    if 4 <= u and u != W_OUT:
                        split_lo(ub + u + 2)
                    if u < W_OUT:
                        dve.wait_ge(unit_used, ub + u + 1)
                    if u < W_K:
                        dve.tensor_tensor(b_q[:, u // 2, :, u % 2, :],
                                          ps[:, u % 7, :].rearrange("p (n t) -> p n t", n=NCH),
                                          rs[:, :].rearrange("p (n t) -> p n t", n=NCH),
                                          ALU.mult).then_inc(b_read, 1)
                    if u == W_K:
                        dve.wait_ge(region_zero, 3 + 2 * KV)
                        for g in range(KV):
                            for par in range(2):
                                src = slice(g * HD, g * HD + HD)
                                dve.scalar_tensor_tensor(out=b_k[g][par][par * HD:par * HD + HD, :],
                                                         in0=ps[src, u % 7, :], scalar=HD ** -0.5,
                                                         in1=rs[src, :], op0=ALU.mult,
                                                         op1=ALU.mult).then_inc(b_read, 1)
                    if u == W_V:
                        dve.tensor_tensor(ta[:, :], ps[:, u % 7, :], rs[:, :], ALU.mult).then_inc(bv_ready, 1)
                        split_lo(ub + W_OUT + 2)
                        for n in range(NCH + 1):
                            if n < NCH:
                                chunk_softmax(n)
                            if n >= 1:
                                chunk_out(s, n - 1)
                    if W_OUT <= u:
                        add_square(16 * s + 8 + u - W_OUT, 0, 0, 2 * s + 1)
                post(s)

            def chunk_softmax(n):
                b = n % 2
                keys = slice(0, CHUNK if n == 0 else P)
                nk = CHUNK if n == 0 else P
                sink = consts[:, C_SINK:C_SINK + 8]
                dve.wait_ge(bs_ready, n + 1)
                scores = ps[:, 2 * b:2 * b + 2, :].rearrange("p a (c k) -> p (a c) k", c=4)[:, :, keys]
                link(dve.tensor_reduce(mx[:, b, :], scores, AX_X, ALU.max))
                link(dve.tensor_tensor(mx[:, b, :], mx[:, b, :], sink, ALU.max))
                dve.tensor_scalar(nmx[:, b, :], mx[:, b, :], -1.0, None, ALU.mult).then_inc(nmx_ready, 1)
                dve.tensor_tensor(smx[:, b, :], sink, mx[:, b, :], ALU.subtract).then_inc(smx_ready, 1)
                dve.wait_ge(p_exp, 9 * (n + 1))
                link(dve.tensor_tensor(den[:, b, :], sm[:, b, :], esk[:, b, :], ALU.add))
                link(dve.reciprocal(rden[:, b, :], den[:, b, :]))
                p = b_p[:, b, :, keys]
                dve.tensor_tensor(p, p, rden[:, b, :].unsqueeze(2).to_broadcast([P, 8, nk]),
                                  ALU.mult).then_inc(p_ready, 1)

            def chunk_out(s, n):
                rows = slice(0, CHUNK if n == 0 else P)
                dve.wait_ge(pt_ready, n + 1)
                if n >= 2:
                    dve.wait_ge(po_ready, n - 1)
                dve.tensor_copy(b_pt[rows, n % 2, 4:8, :],
                                ps[rows, 5, :].rearrange("p (a b) -> p a b", a=4)).then_inc(pt_dve, 1)
                dve.wait_ge(op_hi, KT * OUT_SET[s] + n + 1)
                toks = slice(n * CHUNK, (n + 1) * CHUNK)
                dve.tensor_tensor(x_lo[:, :, toks], ps[:, 6 + n % 2, :].rearrange("p (a b) -> p a b", a=8),
                                  x_hi[:, :, toks].bitcast(F32), ALU.subtract).then_inc(op_lo, 1)

            dve.wait_ge(consts_landed, 16)
            dve.tensor_scalar(half_gain[:, :], consts[:, 0:C_CONVW], 0.5, None, ALU.mult).then_inc(scaled_consts, 1)
            dve.tensor_scalar(gate_b15[:, :], consts[:, C_GATEB:C_GATEB + 1], 1.0 / CAP, None,
                              ALU.mult).then_inc(scaled_consts, 1)
            dve.memset(acc[:, :], 0.0).then_inc(acc_cleared, 1)
            for u in range(3):
                split_lo(u)
            for s, kind in enumerate(STAGES):
                {"ffn": ffn, "mlstm": mlstm, "window": window}[kind](s)
            last = len(STAGES) - 1
            for k in range(KT):
                residual(last, k, y_of(last))

        @block.tensor
        def _(pe):
            def three(dst, w, cols, mv, toks, start, stop, swap=False):
                for n, (a, b) in enumerate(((0, 0), (1, 0), (0, 1))):
                    lhs, rhs = w[a][cols], mv[b][toks]
                    if swap:
                        lhs, rhs = rhs, lhs
                    ins = pe.matmul(dst, lhs, rhs, start=start and n == 0, stop=stop and n == 2)
                return ins

            W, X, H = (w_hi, w_lo), (x_hi, x_lo), (h_hi, h_lo)
            ALL = slice(None)

            def block_cols(c, b, n=P):
                return (ALL, c % RING, slice(b * P, b * P + n))

            def unit(c, m, i, bank):
                pe.wait_ge(lo_split, c + 1 + m * i)
                for k in range(KT):
                    ins = three(ps[:, bank, :], W, block_cols(c, k), X, (ALL, k), k == 0, k == KT - 1)
                ins.then_inc(unit_used, 1)

            def three_units(c, banks, tiles_before, between=None):
                pe.wait_ge(lo_split, c + 3)
                for k in range(KT):
                    pe.wait_ge(op_lo, tiles_before + k + 1)
                    for j in range(3):
                        ins = three(ps[:, banks[j], :], W, block_cols(c + j, k), X, (ALL, k), k == 0, k == KT - 1)
                        if k == KT - 1:
                            ins.then_inc(unit_used, 1)
                    if between:
                        between(k)

            def sum_squares(q):
                pe.wait_ge(acc_done, q)
                for t in range(TT):
                    ins = pe.matmul(ps[:, STAT, t:t + 1], acc[:, t * P:(t + 1) * P], inv_d[:, :], start=True, stop=True)
                ins.then_inc(stat_sum, 1)

            def spread(n, bank, at, done):
                pe.wait_ge(rcol_ready, n + 1)
                for t in range(TT):
                    ins = pe.matmul(ps[:, bank, t * P:(t + 1) * P], rcol[:, at + t:at + t + 1].to_broadcast([P, P]),
                                    ident[:, :], start=True, stop=True)
                ins.then_inc(done, 1)

            def pair(ub, e0, c, m, i, j):
                if not (isinstance(i, int) and e0 + c + j < 2):
                    pe.wait_ge(up_scaled, e0 + c + j - 1 + m * i)
                for half in range(2):
                    unit(ub + 2 * (c + j) + half, 2 * m, i, 2 * (j % 2) + half)

            def ffn(s):
                ub, e0 = BASE[s], FT * FFN_OF[s]
                if e0:
                    pe.wait_ge(up_scaled, e0)
                three_units(ub, (0, 1, 2), KT * SET_OF[s])
                sum_squares(16 * s + 8)
                unit(ub + 3, 0, 0, 3)
                spread(stat_no(s, 0), STAT, 0, bcast_ready)
                with pe.Fori(1, FT // 2) as i:
                    for j in range(2):
                        pair(ub, e0, 0, 2, i, j)
                vb = ub + 2 * FT
                with pe.Fori(0, KT // 4) as i:
                    for d in range(4):
                        at = 0
                        for b, blocks in enumerate(DOWN):
                            c = vb + 3 * d + b
                            pe.wait_ge(lo_split, c + 1 + 12 * i)
                            if b == 0:
                                pe.wait_ge(sq_ready, 16 * s + 8 + d - 1 + 4 * i)
                            for f in range(at, at + blocks):
                                if f in (FT - 2, FT - 1) and d == 0:
                                    pe.wait_ge(hid_lo, e0 + f + 1)
                                elif f == 0 and d == 0:
                                    pe.wait_ge(hid_lo, e0 + FT - 2)
                                ins = three(ps[:, 4 + d % 2, :], W, block_cols(c, f - at), H, (ALL, f),
                                            f == 0, f == FT - 1)
                            at += blocks
                            ins.then_inc(unit_used, 1)
                post(s)

            def post(s):
                sum_squares(16 * s + 16)
                spread(stat_no(s, 1), STAT, 0, bcast_ready)

            def v_unit(ub, first, u):
                c = ub + first + u
                pe.wait_ge(lo_split, c + 1)
                for kk in range(2):
                    k = 2 * u + kk
                    if first == M_V0:
                        pe.wait_ge(op_lo, KT * SET_OF[1] + k + 1)
                    for tt in range(TT):
                        ins = three(ps[:, tt, :], W, (ALL, c % RING, slice(kk * T, kk * T + T)), X,
                                    (ALL, k, slice(tt * P, tt * P + P)), k == 0, k == KT - 1, swap=True)
                ins.then_inc(unit_used, 1)

            def mlstm(s):
                ub = BASE[s]
                pe.wait_ge(up_scaled, FT)
                for u in range(4):
                    v_unit(ub, M_V0, u)
                sum_squares(16 * s + 8)
                unit(ub + M_GATE, 0, 0, 6)
                spread(stat_no(s, 0), STAT, 0, bcast_ready)
                for c in range(KT):
                    if c >= 2:
                        pe.wait_ge(qk_read, c - 1)
                    unit(ub + M_QK + c, 0, 0, 4 + c % 2)
                pe.wait_ge(v_kept, TT)
                for u in range(4):
                    v_unit(ub, M_V1, u)
                pe.wait_ge(gates_done, 2)
                for st in range(TT):
                    ins = pe.matmul(ps[:, 6, st * HEADS:(st + 1) * HEADS], m_e[0:HEADS, 1, st * P:(st + 1) * P],
                                    ident[0:HEADS, 0:HEADS], start=True, stop=True)
                ins.then_inc(acol_sum, 1)
                for c in range(KT):
                    if c >= 2:
                        pe.wait_ge(o_read, c - 1)
                    else:
                        pe.wait_ge(qk_read, KT - 1 + c)
                    unit(ub + M_O + c, 0, 0, 4 + c % 2)
                heads(s)

            def head_scores(h):
                if h == 0:
                    pe.wait_ge(v_kept, 2 * TT)
                    pe.wait_ge(k_placed, KT)
                    pe.wait_ge(o_read, KT)
                else:
                    pe.wait_ge(sc_done, TT * h)
                j, par = divmod(h, 2)
                for st in range(TT):
                    bank, at = ((0, 0), (1, 0), (2, 0), (2, 256))[st]
                    ins = pe.matmul(ps[:, bank, at:at + CAUSAL[st]], m_k[par][:, j, st * P:(st + 1) * P],
                                    m_q[:, j, st * P:T], start=True, stop=True)
                ins.then_inc(s_ready, 1)
                if h:
                    pe.wait_ge(floor_ready, h)
                pick = ident[:, h:h + 1].to_broadcast([P, P])
                pe.matmul(ps[:, 3, :], pick, m_max[:, 0, :], start=True, stop=True)
                pe.matmul(ps[:, 4, :], pick, m_max[:, 1, :], start=True, stop=True).then_inc(maxes_ready, 1)

            def heads(s):
                head_scores(0)
                for h in range(HEADS + 1):
                    if h + 1 < HEADS:
                        head_scores(h + 1)
                    if h < HEADS:
                        pe.wait_ge(sc_done, TT * (h + 1))
                        if h:
                            pe.wait_ge(hs_ready, h)
                        for st in range(TT):
                            ins = pe.matmul(ps[:, 5, P * st:T], m_v[:, st, h * P:(h + 1) * P],
                                            m_sc[:, h % 2, OFF[st]:OFF[st] + CAUSAL[st]],
                                            start=st == 0, stop=st == TT - 1)
                        ins.then_inc(num_ready, 1)
                        for st in range(TT):
                            ins = pe.matmul(ps[:, 6, P * st:T], ones[:, :],
                                            m_sc[:, h % 2, OFF[st]:OFF[st] + CAUSAL[st]],
                                            start=st == 0, stop=st == TT - 1)
                        ins.then_inc(den_ready, 1)
                    if h >= 1:
                        g = h - 1
                        pe.wait_ge(hsq_ready, g + 1)
                        for t in range(TT):
                            ins = pe.matmul(ps[:, STAT, 4 * g + t:4 * g + t + 1], sq[:, h % 2, t * P:(t + 1) * P],
                                            inv_dv[:, :], start=True, stop=True)
                        ins.then_inc(stat_sum if g == HEADS - 1 else stat_heads, 1)
                n = stat_no(s, 0) + 1
                spread(n, 3, 0, head_bcast)
                spread(n, 7, 4, head_bcast)

                def next_head(k):
                    h = k + 2
                    if h < HEADS:
                        pe.wait_ge(og_scaled, k + 1)
                        spread(n, (3, 7)[h % 2], 4 * h, head_bcast)

                out_product(s, M_OUT, next_head)

            def out_product(s, first, between=None):
                ub = BASE[s] + first
                three_units(ub, (4, 5, 6), KT * OUT_SET[s], between)
                for d in range(3, KT):
                    pe.wait_ge(sq_ready, 16 * s + 8 + d - 2)
                    unit(ub + d, 0, 0, 4 + d % 3)
                post(s)

            def window(s):
                ub = BASE[s]
                pe.wait_ge(up_scaled, FT * 3)
                three_units(ub, (0, 1, 2), KT * SET_OF[s])
                sum_squares(16 * s + 8)
                unit(ub + 3, 0, 0, 3)
                spread(stat_no(s, 0), STAT, 0, bcast_ready)
                for u in range(4, W_OUT):
                    if u >= 7:
                        pe.wait_ge(b_read, u - 6)
                    unit(ub + u, 0, 0, u % 7)
                pe.wait_ge(bv_ready, 1)
                pe.wait_ge(b_read, 6)
                for n in range(NCH):
                    nk = CHUNK if n == 0 else P
                    lo = max(n - 1, 0) * CHUNK
                    pe.transpose(ps[0:nk, 4 + n // 4, (n % 4) * P:(n % 4) * P + P], ta[:, lo:lo + nk],
                                 ident[:, :]).then_inc(bw_ready, 1)
                pe.wait_ge(b_read, 8 + 4)
                chunk_scores(0)
                for n in range(NCH):
                    if n + 1 < NCH:
                        chunk_scores(n + 1)
                    chunk_values(n)
                pe.wait_ge(op_lo, KT * (OUT_SET[s] + 1))
                out_product(s, W_OUT)

            def chunk_scores(n):
                nk = CHUNK if n == 0 else P
                lo = max(n - 1, 0) * CHUNK
                if n >= 2:
                    pe.wait_ge(p_exp, 9 * (n - 1))
                for i in range(8):
                    g, par, jp = i // 4, i // 2 % 2, i % 2
                    j = 4 * g + 2 * jp
                    at = (i % 4) * P
                    ins = pe.matmul(ps[:, 2 * (n % 2) + i // 4, at:at + nk],
                                    b_q[:, j // 2, n, :, :].rearrange("p a t -> p (a t)"), b_k[g][par][:, lo:lo + nk],
                                    start=True, stop=True)
                ins.then_inc(bs_ready, 1)

            def chunk_values(n):
                nk = CHUNK if n == 0 else P
                pe.wait_ge(p_ready, n + 1)
                if n == 0:
                    pe.wait_ge(bw_kept, 3)
                else:
                    pe.wait_ge(pt_act, n)
                    pe.wait_ge(pt_dve, n)
                for i in range(8):
                    ins = pe.transpose(ps[0:nk, 4 + i // 4, (i % 4) * P:(i % 4) * P + P],
                                       b_p[:, n % 2, i, 0:nk], ident[:, :])
                ins.then_inc(pt_ready, 1)
                pe.wait_ge(pt_act, n + 1)
                pe.wait_ge(pt_dve, n + 1)
                if n >= 2:
                    pe.wait_ge(op_lo, KT * OUT_SET[4] + n - 1)
                for g in range(KV):
                    for par in range(2):
                        i = 4 * g + 2 * par
                        ins = pe.matmul(ps[par * HD:par * HD + HD, 6 + n % 2, g * 256:(g + 1) * 256],
                                        b_v[0:nk, n, g * HD:(g + 1) * HD], b_pt[0:nk, n % 2, i:i + 2, :],
                                        start=True, stop=True)
                ins.then_inc(po_ready, 1)

            pe.wait_ge(selected, 1)
            pe.wait_ge(zeroed, 6)
            for s, kind in enumerate(STAGES):
                {"ffn": ffn, "mlstm": mlstm, "window": window}[kind](s)


def stat_no(s, post):
    return 2 * s + post + (1 if 2 * s + post > 2 else 0)


def used_out(s, d):
    first = {1: M_OUT, 4: W_OUT}[s]
    return BASE[s] + first + d + 1


def tiles(np, w):
    k, n = w.shape
    return np.ascontiguousarray(
        w.reshape(k // P, P, n // P, P).transpose(2, 1, 0, 3).reshape(n // P, P, k))


def column_tiles(np, v):
    return v.reshape(-1, P).T


def kernel(x, norm_g, ffn_w_gate, ffn_w_up, ffn_w_down, a_w_in, a_conv_w, a_conv_b, a_gate_b, a_head_g,
           a_w_out, b_w_in, b_sinks, b_w_out, c_w_group, c_scale):
    import numpy as np
    import concourse.bacc as bacc
    from concourse.bass_utils import run_bass_kernel_spmd

    f32 = np.float32
    a = {k: np.asarray(v) for k, v in dict(
        x=x, g=norm_g, wg=ffn_w_gate, wu=ffn_w_up, wd=ffn_w_down, aw=a_w_in, cw=a_conv_w, cb=a_conv_b,
        gb=a_gate_b, hg=a_head_g, ao=a_w_out, bw=b_w_in, bs=b_sinks, bo=b_w_out).items()}
    x_t = np.ascontiguousarray(a["x"][0].T.reshape(KT, P, T).transpose(1, 0, 2))
    gate_up = np.stack([np.stack([tiles(np, a["wg"][l, j]), tiles(np, a["wu"][l, j])], 1).reshape(2 * FT, P, UNIT)
                        for l in range(DEPTH) for j in range(2)])
    down = np.stack([tiles(np, a["wd"][l, j]) for l in range(DEPTH) for j in range(2)])
    aw = a["aw"][0]
    qk, v, o, gate = aw[:, 0:D], aw[:, D:2 * D], aw[:, 2 * D:3 * D], aw[:, 3 * D:]
    gates = np.zeros((D, P), f32)
    gates[:, 0:HEADS] = gate[:, 0:HEADS]
    gates[:, 32:32 + HEADS] = gate[:, HEADS:]
    vt = v.reshape(KT // 2, 2, P, 2, T).transpose(3, 0, 2, 1, 4).reshape(KT, P, UNIT)
    mlstm_w = np.concatenate([vt[0:4], tiles(np, gates), tiles(np, qk), vt[4:8], tiles(np, o),
                              tiles(np, a["ao"][0])])
    window_w = np.concatenate([tiles(np, a["bw"][0]), tiles(np, a["bo"][0])])
    gate_b = np.zeros((P, 1), f32)
    gate_b[0:HEADS, 0] = a["gb"][0, 0:HEADS]
    gate_b[32:32 + HEADS, 0] = a["gb"][0, HEADS:]
    conv_w = a["cw"][0].T.reshape(KT, P, TAPS).transpose(1, 0, 2).reshape(P, KT * TAPS)
    sink = a["bs"][0].reshape(KV, 2, 2, 2).transpose(2, 0, 3, 1).reshape(2, 8)
    consts = np.ascontiguousarray(np.concatenate(
        [column_tiles(np, a["g"].reshape(-1)), column_tiles(np, a["hg"][0]), conv_w, column_tiles(np, a["cb"][0]),
         gate_b, np.repeat(sink, HD, axis=0)], axis=1))

    nc = bacc.Bacc("TRN2", target_bir_lowering=False, num_devices=1)
    arrays, args = {}, []
    for name, arr in (("x_t", x_t), ("consts_in", consts), ("gate_up", gate_up), ("down", down),
                      ("mlstm_w", mlstm_w), ("window_w", window_w)):
        arrays[name] = np.ascontiguousarray(arr)
        args.append(nc.dram_tensor(name, arr.shape, mybir.dt.from_np(arr.dtype), kind="ExternalInput").ap())
    args.append(nc.dram_tensor("out_t", (P, KT, T), F32, kind="ExternalOutput").ap())
    build(nc, *args)
    r = run_bass_kernel_spmd(nc, [arrays], core_ids=[0])
    out = r.results[0]["out_t"]
    return np.ascontiguousarray(out.transpose(2, 1, 0).reshape(1, T, D))
```

```python
from contextlib import ExitStack

import concourse.bass as bass
from concourse import mybir

F32 = mybir.dt.float32
F32R = mybir.dt.float32r
ALU = mybir.AluOpType
ACT = mybir.ActivationFunctionType
AX_X = mybir.AxisListType.X

P = 128
T = 512
D = 1024
KT = D // P
TT = T // P
F = 2816
FT = F // P
EPS = 1e-6
CHUNK = 64
NCH = T // CHUNK
DEPTH = 2
NORMS = 6

HEADS = 8
DQK = 64
TAPS = 4
CAP = 15.0

KV = 2
HD = 64

RING = 4
UNIT = 1024
DOWN = (8, 8, 6)

STAGES = ("ffn", "mlstm", "ffn", "ffn", "window", "ffn")
FFN_UNITS = 2 * FT + 3 * KT
M_V0, M_GATE, M_QK, M_V1, M_O, M_OUT, M_UNITS = 0, 4, 5, 13, 17, 25, 33
W_Q, W_K, W_V, W_OUT, W_UNITS = 0, 8, 9, 10, 18
UNITS = {"ffn": FFN_UNITS, "mlstm": M_UNITS, "window": W_UNITS}
BASE = [sum(UNITS[k] for k in STAGES[:s]) for s in range(len(STAGES) + 1)]
FFN_OF = {0: 0, 2: 1, 3: 2, 5: 3}
SET_OF = {0: 0, 1: 1, 2: 3, 3: 4, 4: 5, 5: 7}
OUT_SET = {1: 2, 4: 6}

C_GAIN = 0
C_HEADG = C_GAIN + DEPTH * NORMS * KT
C_CONVW = C_HEADG + HEADS
C_CONVB = C_CONVW + KT * TAPS
C_GATEB = C_CONVB + KT
C_SINK = C_GATEB + 1
C_ALL = C_SINK + 8

STAT = 7
FIRST_BANKS = (4, 5, 6, 3)
DOWN_BANK = (4, 5, 4, 6)

BIG = 3e38


def gain_col(stage, post, k):
    layer, j = divmod(stage, 3)
    return C_GAIN + (layer * NORMS + 2 * j + post) * KT + k


def build(nc, x_t, consts_d, gate_up, down, mlstm_w, window_w, out_t):
    with ExitStack() as ctx:
        def sb(name, shape, dt=F32, to=ctx):
            return to.enter_context(nc.sbuf_tensor(name, shape, dt))

        def sem(name):
            return ctx.enter_context(nc.semaphore(name))

        x = sb("x", [P, KT, T])
        raw = sb("raw", [P, RING, UNIT])
        w_hi = sb("w_hi", [P, RING, UNIT], F32R)
        w_lo = sb("w_lo", [P, RING, UNIT], F32R)
        consts = sb("consts", [P, C_ALL])
        half_gain = sb("half_gain", [P, C_CONVW])
        gate_b15 = sb("gate_b15", [P, 1])
        ident = sb("ident", [P, P])
        ones = sb("ones", [P, P])
        inv_d = sb("inv_d", [P, P])
        inv_dv = sb("inv_dv", [P, P])
        causal = sb("causal", [P, P])
        zeros = sb("zeros", [HEADS, T])
        rs = sb("rs", [P, T])
        acc = sb("acc", [P, T])
        sq = sb("sq", [P, 2, T])
        ms = sb("ms", [P, 4 * HEADS])
        root = sb("root", [P, 4 * HEADS])
        rcol = sb("rcol", [P, 4 * HEADS])
        ta = sb("ta", [P, T])
        tb = sb("tb", [P, T])
        tc = sb("tc", [P, T])
        x_hi = sb("x_hi", [P, KT, T], F32R)
        with ExitStack() as own:
            x_lo = sb("x_lo", [P, KT, T], F32R, own)
        with ExitStack() as own:
            y_ffn = sb("y_ffn", [P, KT, T], F32, own)
        ctx.enter_context(nc.sbuf_tensor("x_lo_room", [P, KT, T], F32))
        with ExitStack() as own:
            h_hi = sb("h_hi", [P, FT, T], F32R, own)
            h_lo = sb("h_lo", [P, FT, T], F32R, own)
        CAUSAL = [T - P * st for st in range(TT)]
        OFF = [sum(CAUSAL[:st]) for st in range(TT)]
        with ExitStack() as own:
            m_q = sb("m_q", [P, KT // 2, T], F32, own)
            m_k = [sb(f"m_k{par}", [P, KT // 2, T], F32, own) for par in range(2)]
            m_o = sb("m_o", [P, KT, T], F32, own)
            m_v = sb("m_v", [P, TT, D], F32, own)
            m_e = sb("m_e", [P, 2, TT, T], F32, own)
            m_sc = sb("m_sc", [P, 2, sum(CAUSAL)], F32, own)
            m_max = sb("m_max", [P, T], F32, own)
        with ExitStack() as own:
            y_mix = sb("y_mix", [P, KT, T], F32, own)
        with ExitStack() as own:
            b_q = sb("b_q", [P, KT // 2, NCH, 2, CHUNK], F32, own)
            b_k = [[sb(f"b_k{g}{par}", [P, T], F32, own) for par in range(2)] for g in range(KV)]
            b_v = sb("b_v", [P, NCH, P], F32, own)
            b_p = sb("b_p", [P, 2, 8, P], F32, own)
            b_pt = sb("b_pt", [P, 2, 8, P], F32, own)
        ctx.enter_context(nc.sbuf_tensor("region", [P, 2 * FT, T], F32))
        u_conv = sb("u_conv", [P, TAPS - 1 + T])
        acol = sb("acol", [P, TT * HEADS])
        floor = sb("floor", [P, HEADS, TT])
        dmag = sb("dmag", [P, 4 * HEADS])
        dneg = sb("dneg", [P, 4 * HEADS])
        dinv = sb("dinv", [P, 4 * HEADS])
        mx = sb("mx", [P, 2, 8])
        nmx = sb("nmx", [P, 2, 8])
        smx = sb("smx", [P, 2, 8])
        esk = sb("esk", [P, 2, 8])
        sm = sb("sm", [P, 2, 8])
        den = sb("den", [P, 2, 8])
        rden = sb("rden", [P, 2, 8])

        ps = ctx.enter_context(nc.psum_tensor("ps", [P, 8, T], F32))

        consts_landed = sem("consts_landed")
        x_landed = [sem(f"x_landed{k}") for k in range(KT)]
        start_landed = [sem(f"start_landed{k}") for k in range(KT + 1)]
        start_hi = sem("start_hi")
        start_lo = sem("start_lo")
        raw_landed = [sem(f"raw_landed{r}") for r in range(RING)]
        out_sent = sem("out_sent")
        hi_split = sem("hi_split")
        lo_split = sem("lo_split")
        unit_used = sem("unit_used")
        zeroed = sem("zeroed")
        selected = sem("selected")
        scaled_consts = sem("scaled_consts")
        op_hi = sem("op_hi")
        op_lo = sem("op_lo")
        sq_ready = sem("sq_ready")
        acc_done = sem("acc_done")
        acc_cleared = sem("acc_cleared")
        stat_sum = sem("stat_sum")
        ms_ready = sem("ms_ready")
        root_ready = sem("root_ready")
        rcol_ready = sem("rcol_ready")
        bcast_ready = sem("bcast_ready")
        rs_ready = sem("rs_ready")
        y_ready = sem("y_ready")
        y_scaled = sem("y_scaled")
        x_new = sem("x_new")
        gate_scaled = sem("gate_scaled")
        up_scaled = sem("up_scaled")
        silu_ready = sem("silu_ready")
        hid_ready = sem("hid_ready")
        hid_hi = sem("hid_hi")
        hid_lo = sem("hid_lo")
        region_zero = sem("region_zero")
        vchain = sem("vchain")
        achain = sem("achain")
        v_kept = sem("v_kept")
        gate_z = sem("gate_z")
        gate_tanh = sem("gate_tanh")
        gate_l = sem("gate_l")
        gates_done = sem("gates_done")
        acol_sum = sem("acol_sum")
        acol_ready = sem("acol_ready")
        qk_read = sem("qk_read")
        conv_ready = sem("conv_ready")
        qk_silu = sem("qk_silu")
        o_read = sem("o_read")
        o_tanh = sem("o_tanh")
        s_ready = sem("s_ready")
        max_ready = sem("max_ready")
        e_ready = sem("e_ready")
        e_masked = sem("e_masked")
        floor_ready = sem("floor_ready")
        sc_done = sem("sc_done")
        num_ready = sem("num_ready")
        den_ready = sem("den_ready")
        hsq_ready = sem("hsq_ready")
        stat_heads = sem("stat_heads")
        og_ready = sem("og_ready")
        head_bcast = sem("head_bcast")
        og_scaled = sem("og_scaled")
        b_read = sem("b_read")
        bv_ready = sem("bv_ready")
        bw_ready = sem("bw_ready")
        bw_kept = sem("bw_kept")
        bs_ready = sem("bs_ready")
        nmx_ready = sem("nmx_ready")
        smx_ready = sem("smx_ready")
        p_exp = sem("p_exp")
        p_ready = sem("p_ready")
        pt_ready = sem("pt_ready")
        pt_act = sem("pt_act")
        pt_dve = sem("pt_dve")
        po_ready = sem("po_ready")

        block = ctx.enter_context(nc.Block())

        @block.sync
        def _(sp):
            sp.dma_start(consts[:, :], consts_d).then_inc(consts_landed, 16)
            for k in range(KT):
                sp.dma_start(x[:, k, :], x_t[:, k, :]).then_inc(x_landed[k], 16)
                cols = slice(k * P, (k + 1) * P)
                sp.dma_start(raw[:, 0:3, cols], gate_up[0, 0:3, :, cols].rearrange("u p c -> p u c")).then_inc(
                    start_landed[k], 16)
            sp.dma_start(raw[:, 3, :], gate_up[0, 3]).then_inc(start_landed[KT], 16)

            def load_unit(c, m, i, src):
                slot = c % RING
                sp.wait_ge(lo_split, c - RING + 1 + m * i)
                sp.dma_start(raw[:, slot, 0:src.shape[-1]], src).then_inc(raw_landed[slot], 16)

            for s, kind in enumerate(STAGES):
                ub = BASE[s]
                if kind == "ffn":
                    n = FFN_OF[s]
                    if s:
                        for u in range(4):
                            load_unit(ub + u, 0, 0, gate_up[n, u])
                    else:
                        sp.wait_ge(lo_split, 3)
                    with sp.Fori(1, FT // 2) as i:
                        for u in range(4):
                            load_unit(ub + u, 4, i, gate_up[n, bass.ds(4 * i + u, 1)].rearrange("a p c -> (a p) c"))
                    with sp.Fori(0, KT // 4) as i:
                        for d in range(4):
                            tile = down[n, bass.ds(4 * i + d, 1)].rearrange("a p c -> (a p) c")
                            at = 0
                            for b, blocks in enumerate(DOWN):
                                load_unit(ub + 2 * FT + 3 * d + b, 12, i, tile[:, at:at + blocks * P])
                                at += blocks * P
                else:
                    src = mlstm_w if kind == "mlstm" else window_w
                    for u in range(UNITS[kind]):
                        load_unit(ub + u, 0, 0, src[u])
            last = len(STAGES) - 1
            for k in range(KT):
                sp.wait_ge(x_new, KT * last + k + 1)
                sp.dma_start(out_t[:, k, :], x[:, k, :]).then_inc(out_sent, 16)
            sp.wait_ge(out_sent, 16 * KT)

        @block.gpsimd
        def _(pool):
            pool.memset(ident[:, :], 0.0).then_inc(zeroed, 1)
            pool.wait_ge(zeroed, 1)
            pool.affine_select(out=ident[:, :], in_=ident[:, :], compare_op=ALU.not_equal, fill=1.0, base=0,
                               pattern=[[-1, P]], channel_multiplier=1).then_inc(selected, 1)
            pool.memset(ones[:, :], 1.0).then_inc(zeroed, 1)
            pool.memset(inv_d[:, :], 1.0 / D).then_inc(zeroed, 1)
            pool.memset(inv_dv[:, :], 1.0 / P).then_inc(zeroed, 1)
            pool.memset(zeros[:, :], 0.0).then_inc(zeroed, 1)
            pool.memset(u_conv[:, 0:TAPS - 1], 0.0).then_inc(zeroed, 1)
            pool.wait_ge(zeroed, 2)
            pool.affine_select(out=causal[:, :], in_=ones[:, :], compare_op=ALU.is_ge, fill=0.0, base=0,
                               pattern=[[1, P]], channel_multiplier=-1).then_inc(selected, 1)

            pool.wait_ge(selected, 2)
            pool.wait_ge(unit_used, BASE[1])
            pool.memset(m_k[0][HD:P, :, :], 0.0).then_inc(region_zero, 1)
            pool.wait_ge(region_zero, 1)
            pool.memset(m_k[1][0:HD, :, :], 0.0).then_inc(region_zero, 1)
            pool.wait_ge(region_zero, 2)
            pool.memset(m_max[:, :], 0.0).then_inc(region_zero, 1)
            pool.wait_ge(unit_used, BASE[4])
            for g in range(KV):
                pool.wait_ge(region_zero, 3 + 2 * g)
                pool.memset(b_k[g][0][HD:P, :], 0.0).then_inc(region_zero, 1)
                pool.wait_ge(region_zero, 3 + 2 * g + 1)
                pool.memset(b_k[g][1][0:HD, :], 0.0).then_inc(region_zero, 1)

        @block.scalar
        def _(act):
            steps = [0]

            def link(ins):
                steps[0] += 1
                ins.then_inc(achain, 1)
                act.wait_ge(achain, steps[0])

            def split_hi(c, m=0, i=0, cols=UNIT):
                slot, u = c % RING, c + m * i
                if isinstance(u, int) and u == RING - 1:
                    act.wait_ge(start_landed[KT], 16)
                else:
                    act.wait_ge(raw_landed[slot], 16 * (c // RING) + 16 * (m // RING) * i)
                    act.wait_ge(unit_used, u - RING + 1)
                act.activation(w_hi[:, slot, 0:cols], raw[:, slot, 0:cols], ACT.Copy).then_inc(hi_split, 1)

            def square(q, m, i, src):
                if q >= 2:
                    act.wait_ge(acc_done, q - 1 + m * i)
                act.activation(sq[:, q % 2, :], src, ACT.Square).then_inc(sq_ready, 1)

            def input_tiles(s):
                for k in range(KT):
                    if s == 0:
                        act.wait_ge(start_landed[k], 16)
                        cols = slice(k * P, (k + 1) * P)
                        act.activation(w_hi[:, 0:3, cols], raw[:, 0:3, cols], ACT.Copy).then_inc(
                            *((start_hi, 1) if k < KT - 3 else (hi_split, 1)))
                        act.wait_ge(x_landed[k], 16)
                        if k == 0:
                            act.wait_ge(consts_landed, 16)
                    else:
                        act.wait_ge(x_new, KT * (s - 1) + k + 1)
                    g = gain_col(s, 0, k)
                    act.activation(x_hi[:, k, :], x[:, k, :], ACT.Copy, scale=consts[:, g:g + 1]).then_inc(op_hi, 1)
                    if k < 2:
                        input_square(s, k)
                if s == 0:
                    split_hi(RING - 1)

            def input_square(s, k):
                square(16 * s + k, 0, 0, x[:, k, :])

            def input_squares(s):
                for k in range(2, KT):
                    if k == KT // 2:
                        split_hi(BASE[s] + 4)
                    input_square(s, k)
                split_hi(BASE[s] + 5)

            def sqrt_stat(n, cols=TT):
                act.wait_ge(ms_ready, n + 1)
                act.activation(root[:, 0:cols], ms[:, 0:cols], ACT.Sqrt).then_inc(root_ready, 1)

            def keep_rs(s):
                act.wait_ge(bcast_ready, 2 * s + 1)
                act.activation(rs[:, :], ps[:, STAT, :], ACT.Copy).then_inc(rs_ready, 1)

            def output_tile(s, c, m, i, bank, gain, y, used):
                act.wait_ge(unit_used, used)
                d = c + m * i
                col = gain_col(s, 1, 0) + d
                dst = y[:, bass.ds(d, 1), :].rearrange("p a t -> p (a t)")
                last = c == (3 if m else KT - 1)
                if last:
                    square(16 * s + 8 + c, m, i, ps[:, bank, :])
                act.activation(dst, ps[:, bank, :], ACT.Copy, scale=gain[:, bass.ds(col, 1)]).then_inc(y_ready, 1)
                if not last:
                    square(16 * s + 8 + c, m, i, ps[:, bank, :])

            def hidden(e, c, m, i):
                act.wait_ge(gate_scaled, e + m * i + 1)
                act.activation(tc[:, :], ta[:, :], ACT.Silu).then_inc(silu_ready, 1)
                act.wait_ge(hid_ready, e + m * i + 1)
                dst = h_hi[:, bass.ds(c + m * i, 1), :].rearrange("p a t -> p (a t)")
                act.activation(dst, tb[:, :], ACT.Copy).then_inc(hid_hi, 1)

            def ffn(s):
                ub, e0 = BASE[s], FT * FFN_OF[s]
                input_tiles(s)
                input_squares(s)
                split_hi(ub + 6)
                sqrt_stat(stat_no(s, 0))
                split_hi(ub + 7)
                keep_rs(s)
                for c in range(4):
                    if c == 3:
                        split_hi(ub + 8)
                        split_hi(ub + 9)
                    hidden(e0 + c, c, 0, 0)
                with act.Fori(2, FT // 2) as i:
                    for j in range(2):
                        split_hi(ub + 2 * j + 2, 4, i)
                        split_hi(ub + 2 * j + 3, 4, i)
                        hidden(e0 + j, j, 2, i)
                vb = ub + 2 * FT
                split_hi(vb + 2, 0, 0, DOWN[2] * P)

                def four_tiles(i, splits=12):
                    for d in range(4):
                        for b in range(3):
                            if 3 * d + b < splits:
                                split_hi(vb + 3 * d + b + 3, 12, i, UNIT if d == 3 else DOWN[b] * P)
                        output_tile(s, d, 4, i, DOWN_BANK[d], half_gain, y_ffn, vb + 3 * d + 3 + 12 * i)

                last = s + 1 == len(STAGES)
                with act.Fori(0, KT // 4 - last) as i:
                    four_tiles(i)
                if last:
                    four_tiles(KT // 4 - 1, 9)
                post(s)

            def post(s):
                sqrt_stat(stat_no(s, 1))
                if s + 1 < len(STAGES):
                    split_hi(BASE[s + 1] + 3)

            def mlstm(s):
                ub = BASE[s]
                input_tiles(s)
                input_squares(s)
                for u in range(M_UNITS):
                    if u == M_GATE:
                        split_hi(ub + M_GATE + 2)
                        sqrt_stat(stat_no(s, 0))
                        split_hi(ub + M_GATE + 3)
                        keep_rs(s)
                        keep_v(0)
                    if M_GATE < u:
                        split_hi(ub + u + 3)
                    if u == M_GATE:
                        act.wait_ge(gate_z, 1)
                        act.activation(tc[0:40, :], ta[0:40, :], ACT.Tanh, bias=gate_b15[0:40, :],
                                       scale=1.0 / CAP).then_inc(gate_tanh, 1)
                        act.wait_ge(gate_tanh, 1)
                        link(act.activation(tb[0:HEADS, :], tc[32:40, :], ACT.Exp, scale=-CAP))
                        act.activation(m_e[0:HEADS, 0, 1, :], tb[0:HEADS, :], ACT.Ln,
                                       bias=ones[0:HEADS, 0:1]).then_inc(gate_l, 1)
                    if M_QK <= u < M_QK + KT:
                        c = u - M_QK
                        act.wait_ge(conv_ready, c + 1)
                        src = (ta, tb)[c % 2]
                        if c < KT // 2:
                            act.activation(m_q[:, c, :], src[:, :], ACT.Silu).then_inc(qk_silu, 1)
                        else:
                            act.activation(m_k[0][0:HD, c - KT // 2, :], src[0:HD, :], ACT.Silu)
                            act.activation(m_k[1][HD:P, c - KT // 2, :], src[HD:P, :],
                                           ACT.Silu).then_inc(qk_silu, 1)
                    if u == M_V1 + 3:
                        keep_v(1)
                    if M_O <= u < M_O + KT:
                        c = u - M_O
                        act.wait_ge(o_read, c + 1)
                        act.activation(m_o[:, c, :], (ta, tb)[c % 2][:, :], ACT.Tanh, scale=0.5).then_inc(o_tanh, 1)
                    if u == M_OUT - 1:
                        heads(s)
                    if M_OUT <= u:
                        d = u - M_OUT
                        output_tile(s, d, 0, 0, 4 + d % 3, consts, y_mix, used_out(s, d))
                post(s)

            def keep_v(half):
                act.wait_ge(unit_used, BASE[1] + (M_V0 if half == 0 else M_V1) + 4)
                act.wait_ge(rcol_ready, stat_no(1, 0) + 1)
                for tt in range(TT):
                    act.activation(m_v[:, tt, half * T:half * T + T], ps[:, tt, :], ACT.Copy,
                                   scale=rcol[:, tt:tt + 1]).then_inc(v_kept, 1)

            def heads(s):
                act.wait_ge(acol_ready, 1)
                act.activation(floor[:, :, :].rearrange("p h t -> p t h"),
                               ps[:, 6, TT * HEADS:2 * TT * HEADS].rearrange("p (t h) -> p t h", t=TT),
                               ACT.Exp).then_inc(floor_ready, 1)
                for h in range(HEADS + 1):
                    if h < HEADS:
                        act.wait_ge(max_ready, h + 1)
                        if h >= 2:
                            act.wait_ge(sc_done, TT * (h - 1))
                        for st in range(TT):
                            act.activation(m_e[:, h % 2, st, 0:CAUSAL[st]], ps[:, 3 + h % 2, P * st:T], ACT.Exp,
                                           bias=acol[:, st * HEADS + h:st * HEADS + h + 1]).then_inc(e_ready, 1)
                    if h >= 1:
                        act.wait_ge(num_ready, h)
                        if h >= 3:
                            act.wait_ge(stat_heads, h - 2)
                        act.activation(sq[:, h % 2, :], ps[:, 5 + (h - 1) % 2, :], ACT.Square).then_inc(hsq_ready, 1)
                sqrt_stat(stat_no(1, 0) + 1, 4 * HEADS)
                for h in range(HEADS):
                    act.wait_ge(og_scaled, h + 1)
                    act.activation(x_hi[:, h, :], m_o[:, h, :], ACT.Copy,
                                   scale=half_gain[:, C_HEADG + h:C_HEADG + h + 1]).then_inc(op_hi, 1)

            def window(s):
                ub = BASE[s]
                input_tiles(s)
                input_squares(s)
                split_hi(ub + 6)
                sqrt_stat(stat_no(s, 0))
                split_hi(ub + 7)
                keep_rs(s)
                for u in range(W_UNITS):
                    if u > 4:
                        split_hi(ub + u + 3)
                    if u == W_V:
                        act.wait_ge(bw_ready, 8)
                        act.activation(b_v[0:CHUNK, 0, :], ps[0:CHUNK, 4, 0:P], ACT.Copy).then_inc(bw_kept, 1)
                        act.activation(b_v[:, 1:4, :], ps[:, 4, P:T].rearrange("p (a b) -> p a b", a=3),
                                       ACT.Copy).then_inc(bw_kept, 1)
                        act.activation(b_v[:, 4:8, :], ps[:, 5, :].rearrange("p (a b) -> p a b", a=4),
                                       ACT.Copy).then_inc(bw_kept, 1)
                        chunk_exp(0)
                        for n in range(NCH + 1):
                            if n + 1 < NCH:
                                chunk_exp(n + 1)
                            if n >= 1:
                                chunk_round(n - 1)
                            if n < NCH:
                                chunk_turn(n)
                    if W_OUT <= u:
                        d = u - W_OUT
                        output_tile(s, d, 0, 0, 4 + d % 3, consts, y_mix, used_out(s, d))
                post(s)

            def chunk_exp(n):
                keys = slice(0, CHUNK if n == 0 else P)
                act.wait_ge(nmx_ready, n + 1)
                if n >= 2:
                    act.wait_ge(pt_ready, n - 1)
                for i in range(8):
                    act.activation(b_p[:, n % 2, i, keys], ps[:, 2 * (n % 2) + i // 4, :].rearrange(
                        "p (a b) -> p a b", a=4)[:, i % 4, keys], ACT.Exp, bias=nmx[:, n % 2, i:i + 1],
                        accum_out=sm[:, n % 2, i:i + 1]).then_inc(p_exp, 1)
                act.wait_ge(smx_ready, n + 1)
                act.activation(esk[:, n % 2, :], smx[:, n % 2, :], ACT.Exp).then_inc(p_exp, 1)

            def chunk_turn(n):
                rows = slice(0, CHUNK if n == 0 else P)
                act.wait_ge(pt_ready, n + 1)
                if n >= 2:
                    act.wait_ge(po_ready, n - 1)
                act.activation(b_pt[rows, n % 2, 0:4, :], ps[rows, 4, :].rearrange("p (a b) -> p a b", a=4),
                               ACT.Copy).then_inc(pt_act, 1)

            def chunk_round(n):
                act.wait_ge(po_ready, n + 1)
                act.activation(x_hi[:, :, n * CHUNK:(n + 1) * CHUNK],
                               ps[:, 6 + n % 2, :].rearrange("p (a b) -> p a b", a=8), ACT.Copy).then_inc(op_hi, 1)

            for s, kind in enumerate(STAGES):
                {"ffn": ffn, "mlstm": mlstm, "window": window}[kind](s)

        @block.vector
        def _(dve):
            steps = [0]

            def link(ins):
                steps[0] += 1
                ins.then_inc(vchain, 1)
                dve.wait_ge(vchain, steps[0])

            def split_lo(c, m=0, i=0, cols=UNIT):
                slot, u = c % RING, c + m * i
                dve.wait_ge(hi_split, u + 1)
                dve.tensor_tensor(w_lo[:, slot, 0:cols], raw[:, slot, 0:cols], w_hi[:, slot, 0:cols].bitcast(F32),
                                  ALU.subtract).then_inc(lo_split, 1)

            def add_square(q, m, i, n):
                dve.wait_ge(acc_cleared, n + 1)
                if q >= 1:
                    dve.wait_ge(acc_done, q + m * i)
                dve.wait_ge(sq_ready, q + m * i + 1)
                dve.tensor_tensor(acc[:, :], acc[:, :], sq[:, q % 2, :], ALU.add).then_inc(acc_done, 1)

            def input_lo(s, k):
                g = gain_col(s, 0, k)
                if s == 0:
                    cols = slice(k * P, (k + 1) * P)
                    if k < KT - 3:
                        dve.wait_ge(start_hi, k + 1)
                    else:
                        dve.wait_ge(hi_split, k - (KT - 3) + 1)
                    dve.tensor_tensor(w_lo[:, 0:3, cols], raw[:, 0:3, cols], w_hi[:, 0:3, cols].bitcast(F32),
                                      ALU.subtract).then_inc(*((start_lo, 1) if k < KT - 3 else (lo_split, 1)))
                dve.wait_ge(op_hi, KT * SET_OF[s] + k + 1)
                dve.scalar_tensor_tensor(out=x_lo[:, k, :], in0=x[:, k, :], scalar=consts[:, g:g + 1],
                                         in1=x_hi[:, k, :].bitcast(F32), op0=ALU.mult,
                                         op1=ALU.subtract).then_inc(op_lo, 1)

            def scale_y(s, k, y):
                dve.wait_ge(bcast_ready, 2 * s + 2)
                dve.wait_ge(y_ready, KT * s + k + 1)
                dve.tensor_tensor(y[:, k, :], y[:, k, :], ps[:, STAT, :], ALU.mult).then_inc(y_scaled, 1)

            def add_y(s, k, y):
                dve.wait_ge(y_scaled, KT * s + k + 1)
                dve.tensor_tensor(x[:, k, :], x[:, k, :], y[:, k, :], ALU.add).then_inc(x_new, 1)

            def input_tiles(s):
                if s == 0:
                    for k in range(KT):
                        input_lo(s, k)
                    split_lo(RING - 1)
                    return
                y = y_of(s - 1)
                for k in range(KT + 1):
                    if k < KT:
                        scale_y(s - 1, k, y)
                    if k >= 1:
                        input_lo(s, k - 1)
                    if k < KT:
                        add_y(s - 1, k, y)

            def input_squares(s):
                for k in range(KT):
                    if k == KT // 2:
                        split_lo(BASE[s] + 4)
                    add_square(16 * s + k, 0, 0, 2 * s)
                split_lo(BASE[s] + 5)

            def y_of(s):
                return y_ffn if s >= 0 and STAGES[s] == "ffn" else y_mix

            def stat_ms(n):
                dve.wait_ge(stat_sum, n + 1)
                dve.tensor_scalar(ms[:, 0:TT], ps[:, STAT, 0:TT], EPS, None, ALU.add).then_inc(ms_ready, 1)
                dve.memset(acc[:, :], 0.0).then_inc(acc_cleared, 1)

            def stat_rcol(n, cols=TT):
                dve.wait_ge(root_ready, n + 1)
                dve.reciprocal(rcol[:, 0:cols], root[:, 0:cols]).then_inc(rcol_ready, 1)

            def hidden(e, ub, c, m, i, banks=None):
                n = e + m * i
                gate, up = banks or (2 * (c % 2), 2 * (c % 2) + 1)
                dve.wait_ge(unit_used, ub + 2 * c + 1 + 2 * m * i)
                dve.tensor_tensor(ta[:, :], ps[:, gate, :], rs[:, :], ALU.mult).then_inc(gate_scaled, 1)
                dve.wait_ge(unit_used, ub + 2 * c + 2 + 2 * m * i)
                if e or not isinstance(i, int):
                    dve.wait_ge(hid_lo, n)
                dve.tensor_tensor(tb[:, :], ps[:, up, :], rs[:, :], ALU.mult).then_inc(up_scaled, 1)
                dve.wait_ge(up_scaled, n + 1)
                dve.wait_ge(silu_ready, n + 1)
                dve.tensor_tensor(tb[:, :], tb[:, :], tc[:, :], ALU.mult).then_inc(hid_ready, 1)
                dve.wait_ge(hid_hi, n + 1)
                f = bass.ds(c + m * i, 1)
                dve.tensor_tensor(h_lo[:, f, :].rearrange("p a t -> p (a t)"), tb[:, :],
                                  h_hi[:, f, :].rearrange("p a t -> p (a t)").bitcast(F32),
                                  ALU.subtract).then_inc(hid_lo, 1)

            def ffn(s):
                ub, e0 = BASE[s], FT * FFN_OF[s]
                input_tiles(s)
                input_squares(s)
                split_lo(ub + 6)
                stat_ms(stat_no(s, 0))
                stat_rcol(stat_no(s, 0))
                split_lo(ub + 7)
                dve.wait_ge(rs_ready, s + 1)
                for c in range(4):
                    if c == 3:
                        split_lo(ub + 8)
                        split_lo(ub + 9)
                    hidden(e0 + c, ub, c, 0, 0, FIRST_BANKS[2 * c:2 * c + 2])
                with dve.Fori(2, FT // 2) as i:
                    for j in range(2):
                        split_lo(ub + 2 * j + 2, 4, i)
                        split_lo(ub + 2 * j + 3, 4, i)
                        hidden(e0 + j, ub, j, 2, i)
                vb = ub + 2 * FT
                split_lo(vb + 2, 0, 0, DOWN[2] * P)

                def four_tiles(i, splits=12):
                    for d in range(4):
                        for b in range(3):
                            if 3 * d + b < splits:
                                split_lo(vb + 3 * d + b + 3, 12, i, UNIT if d == 3 else DOWN[b] * P)
                        add_square(16 * s + 8 + d, 4, i, 2 * s + 1)

                last = s + 1 == len(STAGES)
                with dve.Fori(0, KT // 4 - last) as i:
                    four_tiles(i)
                if last:
                    four_tiles(KT // 4 - 1, 9)
                post(s)

            def post(s):
                stat_ms(stat_no(s, 1))
                stat_rcol(stat_no(s, 1))
                if s + 1 < len(STAGES):
                    split_lo(BASE[s + 1] + 3)

            def mlstm(s):
                ub = BASE[s]
                input_tiles(s)
                input_squares(s)
                for u in range(M_UNITS):
                    if u == M_GATE:
                        split_lo(ub + M_GATE + 2)
                        stat_ms(stat_no(s, 0))
                        stat_rcol(stat_no(s, 0))
                        split_lo(ub + M_GATE + 3)
                    if M_GATE < u:
                        split_lo(ub + u + 3)
                    if u == M_GATE:
                        gates(ub)
                    if M_QK <= u < M_QK + KT:
                        qk_tile(ub, u, u - M_QK)
                    if u == M_V1 + 3:
                        dve.wait_ge(acol_sum, 1)
                        dve.tensor_copy(acol[:, :], ps[:, 6, 0:TT * HEADS]).then_inc(acol_ready, 1)
                    if M_O <= u < M_O + KT:
                        c = u - M_O
                        dve.wait_ge(unit_used, ub + u + 1)
                        if c >= 2:
                            dve.wait_ge(o_tanh, c - 1)
                        else:
                            dve.wait_ge(qk_silu, KT)
                        dve.tensor_tensor((ta, tb)[c % 2][:, :], ps[:, 4 + c % 2, :], rs[:, :],
                                          ALU.mult).then_inc(o_read, 1)
                    if u == M_OUT - 1:
                        heads(s)
                    if M_OUT <= u:
                        add_square(16 * s + 8 + u - M_OUT, 0, 0, 2 * s + 1)
                post(s)

            def gates(ub):
                dve.wait_ge(unit_used, ub + M_GATE + 1)
                dve.wait_ge(rs_ready, 2)
                dve.tensor_tensor(ta[0:40, :], ps[0:40, 6, :], rs[0:40, :], ALU.mult).then_inc(gate_z, 1)
                dve.wait_ge(gate_l, 1)
                run, soft, a, top = (m_e[0:HEADS, 0, j, :] for j in range(4))
                dve.wait_ge(zeroed, 6)
                link(dve.tensor_tensor_scan(run, zeros[:, :], soft, 0.0, ALU.add, ALU.add))
                link(dve.scalar_tensor_tensor(out=a, in0=tc[0:HEADS, :], scalar=CAP, in1=run, op0=ALU.mult,
                                              op1=ALU.add))
                link(dve.tensor_tensor_scan(top, zeros[:, :], a, 0.0, ALU.add, ALU.max))
                dve.wait_ge(region_zero, 3)
                dve.tensor_scalar(m_max[0:HEADS, :], top, -1.0, None, ALU.mult).then_inc(gates_done, 1)
                dve.tensor_tensor(m_e[0:HEADS, 1, 0, :], run, top, ALU.subtract).then_inc(gates_done, 1)

            def qk_tile(ub, u, c):
                dve.wait_ge(unit_used, ub + u + 1)
                dve.tensor_tensor(u_conv[:, TAPS - 1:], ps[:, 4 + c % 2, :], rs[:, :], ALU.mult).then_inc(qk_read, 1)
                dve.wait_ge(qk_read, c + 1)
                buf = (ta, tb)[c % 2][:, :]
                if c >= 2:
                    dve.wait_ge(qk_silu, c - 1)
                w = C_CONVW + c * TAPS
                for j in range(TAPS):
                    if j == 0:
                        ins = dve.tensor_scalar(buf, u_conv[:, 0:T], consts[:, w:w + 1],
                                                consts[:, C_CONVB + c:C_CONVB + c + 1], ALU.mult, ALU.add)
                    else:
                        ins = dve.scalar_tensor_tensor(out=buf, in0=u_conv[:, j:j + T],
                                                       scalar=consts[:, w + j:w + j + 1], in1=buf,
                                                       op0=ALU.mult, op1=ALU.add)
                    if j < TAPS - 1:
                        link(ins)
                    else:
                        ins.then_inc(conv_ready, 1)

            def heads(s):
                for h in range(HEADS + 1):
                    if h < HEADS:
                        dve.wait_ge(e_ready, TT * (h + 1))
                        diag = m_e[:, h % 2, :, 0:P]
                        dve.wait_ge(selected, 2)
                        dve.scalar_tensor_tensor(out=diag, in0=diag, scalar=BIG,
                                                 in1=causal[:, :].unsqueeze(1).to_broadcast([P, TT, P]),
                                                 op0=ALU.min, op1=ALU.mult).then_inc(e_masked, 1)
                        dve.wait_ge(e_masked, h + 1)
                        dve.wait_ge(s_ready, h + 1)
                        if h >= 2:
                            dve.wait_ge(den_ready, h - 1)
                        for st in range(TT):
                            bank, at = ((0, 0), (1, 0), (2, 0), (2, 256))[st]
                            dve.scalar_tensor_tensor(out=m_sc[:, h % 2, OFF[st]:OFF[st] + CAUSAL[st]],
                                                     in0=ps[:, bank, at:at + CAUSAL[st]], scalar=DQK ** -0.5,
                                                     in1=m_e[:, h % 2, st, 0:CAUSAL[st]], op0=ALU.mult,
                                                     op1=ALU.mult).then_inc(sc_done, 1)
                    if h >= 1:
                        g = h - 1
                        dve.wait_ge(hsq_ready, g + 1)
                        dve.scalar_tensor_tensor(out=m_o[:, g, :], in0=m_o[:, g, :], scalar=1.0,
                                                 in1=ps[:, 5 + g % 2, :], op0=ALU.add,
                                                 op1=ALU.mult).then_inc(og_ready, 1)
                n = stat_no(1, 0) + 1
                dve.wait_ge(stat_sum, n + 1)
                dve.wait_ge(floor_ready, 1)
                link(dve.tensor_copy(dmag[:, :], ps[:, STAT, 0:4 * HEADS]))
                link(dve.tensor_scalar(dneg[:, :], dmag[:, :], -1.0, None, ALU.mult))
                link(dve.tensor_tensor(dmag[:, :], dmag[:, :], dneg[:, :], ALU.max))
                link(dve.tensor_tensor(dmag[:, :], dmag[:, :], floor[:, :, :].rearrange("p h t -> p (h t)"), ALU.max))
                link(dve.reciprocal(dinv[:, :], dmag[:, :]))
                link(dve.tensor_tensor(dneg[:, :], dinv[:, :], ps[:, STAT, 256:256 + 4 * HEADS], ALU.mult))
                link(dve.tensor_tensor(dneg[:, :], dneg[:, :], dinv[:, :], ALU.mult))
                dve.tensor_scalar(ms[:, :], dneg[:, :], EPS, None, ALU.add).then_inc(ms_ready, 1)
                dve.wait_ge(root_ready, n + 1)
                link(dve.reciprocal(dneg[:, :], root[:, :]))
                dve.tensor_tensor(rcol[:, :], dneg[:, :], dinv[:, :], ALU.mult).then_inc(rcol_ready, 1)
                for h in range(HEADS + 1):
                    if h < HEADS:
                        dve.wait_ge(head_bcast, h + 1)
                        dve.wait_ge(og_ready, h + 1)
                        dve.tensor_tensor(m_o[:, h, :], m_o[:, h, :], ps[:, (3, 7)[h % 2], :],
                                          ALU.mult).then_inc(og_scaled, 1)
                    if h >= 1:
                        g = h - 1
                        dve.wait_ge(op_hi, KT * OUT_SET[s] + g + 1)
                        dve.wait_ge(og_scaled, g + 1)
                        col = C_HEADG + g
                        dve.scalar_tensor_tensor(out=x_lo[:, g, :], in0=m_o[:, g, :],
                                                 scalar=half_gain[:, col:col + 1],
                                                 in1=x_hi[:, g, :].bitcast(F32), op0=ALU.mult,
                                                 op1=ALU.subtract).then_inc(op_lo, 1)

            def window(s):
                ub = BASE[s]
                input_tiles(s)
                input_squares(s)
                split_lo(ub + 6)
                stat_ms(stat_no(s, 0))
                stat_rcol(stat_no(s, 0))
                split_lo(ub + 7)
                dve.wait_ge(rs_ready, s + 1)
                for u in range(W_UNITS):
                    if u > 4:
                        split_lo(ub + u + 3)
                    if u < W_OUT:
                        dve.wait_ge(unit_used, ub + u + 1)
                    if u < W_K:
                        dve.tensor_tensor(b_q[:, u // 2, :, u % 2, :],
                                          ps[:, u % 7, :].rearrange("p (n t) -> p n t", n=NCH),
                                          rs[:, :].rearrange("p (n t) -> p n t", n=NCH),
                                          ALU.mult).then_inc(b_read, 1)
                    if u == W_K:
                        dve.wait_ge(region_zero, 3 + 2 * KV)
                        for g in range(KV):
                            for par in range(2):
                                src = slice(g * HD, g * HD + HD)
                                dve.scalar_tensor_tensor(out=b_k[g][par][par * HD:par * HD + HD, :],
                                                         in0=ps[src, u % 7, :], scalar=HD ** -0.5,
                                                         in1=rs[src, :], op0=ALU.mult,
                                                         op1=ALU.mult).then_inc(b_read, 1)
                    if u == W_V:
                        dve.tensor_tensor(ta[:, :], ps[:, u % 7, :], rs[:, :], ALU.mult).then_inc(bv_ready, 1)
                        chunk_max(0)
                        for n in range(NCH + 1):
                            if n + 1 < NCH:
                                chunk_max(n + 1)
                            if n < NCH:
                                chunk_divide(n)
                            if n >= 1:
                                chunk_rest(s, n - 1)
                            if n < NCH:
                                chunk_turn(n)
                    if W_OUT <= u:
                        add_square(16 * s + 8 + u - W_OUT, 0, 0, 2 * s + 1)
                post(s)

            def chunk_max(n):
                b = n % 2
                keys = slice(0, CHUNK if n == 0 else P)
                sink = consts[:, C_SINK:C_SINK + 8]
                dve.wait_ge(bs_ready, n + 1)
                scores = ps[:, 2 * b:2 * b + 2, :].rearrange("p a (c k) -> p (a c) k", c=4)[:, :, keys]
                link(dve.tensor_reduce(mx[:, b, :], scores, AX_X, ALU.max))
                link(dve.tensor_tensor(mx[:, b, :], mx[:, b, :], sink, ALU.max))
                dve.tensor_scalar(nmx[:, b, :], mx[:, b, :], -1.0, None, ALU.mult).then_inc(nmx_ready, 1)
                dve.tensor_tensor(smx[:, b, :], sink, mx[:, b, :], ALU.subtract).then_inc(smx_ready, 1)

            def chunk_divide(n):
                b = n % 2
                nk = CHUNK if n == 0 else P
                keys = slice(0, nk)
                dve.wait_ge(p_exp, 9 * (n + 1))
                link(dve.tensor_tensor(den[:, b, :], sm[:, b, :], esk[:, b, :], ALU.add))
                link(dve.reciprocal(rden[:, b, :], den[:, b, :]))
                p = b_p[:, b, :, keys]
                dve.tensor_tensor(p, p, rden[:, b, :].unsqueeze(2).to_broadcast([P, 8, nk]),
                                  ALU.mult).then_inc(p_ready, 1)

            def chunk_turn(n):
                rows = slice(0, CHUNK if n == 0 else P)
                dve.wait_ge(pt_ready, n + 1)
                if n >= 2:
                    dve.wait_ge(po_ready, n - 1)
                dve.tensor_copy(b_pt[rows, n % 2, 4:8, :],
                                ps[rows, 5, :].rearrange("p (a b) -> p a b", a=4)).then_inc(pt_dve, 1)

            def chunk_rest(s, n):
                dve.wait_ge(op_hi, KT * OUT_SET[s] + n + 1)
                toks = slice(n * CHUNK, (n + 1) * CHUNK)
                dve.tensor_tensor(x_lo[:, :, toks], ps[:, 6 + n % 2, :].rearrange("p (a b) -> p a b", a=8),
                                  x_hi[:, :, toks].bitcast(F32), ALU.subtract).then_inc(op_lo, 1)

            dve.wait_ge(consts_landed, 16)
            dve.tensor_scalar(half_gain[:, :], consts[:, 0:C_CONVW], 0.5, None, ALU.mult).then_inc(scaled_consts, 1)
            dve.tensor_scalar(gate_b15[:, :], consts[:, C_GATEB:C_GATEB + 1], 1.0 / CAP, None,
                              ALU.mult).then_inc(scaled_consts, 1)
            dve.memset(acc[:, :], 0.0).then_inc(acc_cleared, 1)
            for s, kind in enumerate(STAGES):
                {"ffn": ffn, "mlstm": mlstm, "window": window}[kind](s)
            last = len(STAGES) - 1
            for k in range(KT):
                scale_y(last, k, y_of(last))
                add_y(last, k, y_of(last))

        @block.tensor
        def _(pe):
            def three(dst, w, cols, mv, toks, start, stop, swap=False):
                for n, (a, b) in enumerate(((0, 0), (1, 0), (0, 1))):
                    lhs, rhs = w[a][cols], mv[b][toks]
                    if swap:
                        lhs, rhs = rhs, lhs
                    ins = pe.matmul(dst, lhs, rhs, start=start and n == 0, stop=stop and n == 2)
                return ins

            W, X, H = (w_hi, w_lo), (x_hi, x_lo), (h_hi, h_lo)
            ALL = slice(None)

            def block_cols(c, b, n=P):
                return (ALL, c % RING, slice(b * P, b * P + n))

            def unit(c, m, i, bank, midway=None):
                pe.wait_ge(lo_split, c + 1 + m * i)
                for k in range(KT):
                    if midway and k == KT // 2:
                        midway()
                    ins = three(ps[:, bank, :], W, block_cols(c, k), X, (ALL, k), k == 0, k == KT - 1)
                ins.then_inc(unit_used, 1)

            def three_units(c, banks, tiles_before, between=None):
                if c:
                    pe.wait_ge(lo_split, c + 3)
                for k in range(KT):
                    if c == 0:
                        if k < KT - 3:
                            pe.wait_ge(start_lo, k + 1)
                        else:
                            pe.wait_ge(lo_split, k - (KT - 3) + 1)
                    pe.wait_ge(op_lo, tiles_before + k + 1)
                    for j in range(3):
                        ins = three(ps[:, banks[j], :], W, block_cols(c + j, k), X, (ALL, k), k == 0, k == KT - 1)
                        if k == KT - 1:
                            ins.then_inc(unit_used, 1)
                    if between:
                        between(k)

            def sum_squares(q):
                pe.wait_ge(acc_done, q)
                for t in range(TT):
                    ins = pe.matmul(ps[:, STAT, t:t + P], acc[:, t * P:(t + 1) * P], inv_d[:, :],
                                    start=True, stop=True)
                ins.then_inc(stat_sum, 1)

            def spread(n, bank, at, done):
                pe.wait_ge(rcol_ready, n + 1)
                for t in range(TT):
                    ins = pe.matmul(ps[:, bank, t * P:(t + 1) * P], rcol[:, at + t:at + t + 1].to_broadcast([P, P]),
                                    ident[:, :], start=True, stop=True)
                ins.then_inc(done, 1)

            def pair(ub, e0, c, m, i, j):
                pe.wait_ge(up_scaled, e0 + c + j - 1 + m * i)
                for half in range(2):
                    unit(ub + 2 * (c + j) + half, 2 * m, i, 2 * (j % 2) + half)

            def fourth(c, bank, k):
                if k == 0:
                    pe.wait_ge(lo_split, c + 1)
                ins = three(ps[:, bank, :], W, block_cols(c, k), X, (ALL, k), k == 0, k == KT - 1)
                if k == KT - 1:
                    ins.then_inc(unit_used, 1)

            def begin(s, banks):
                ub = BASE[s]
                behind = 2 if s else KT

                def between(k):
                    if k >= behind:
                        fourth(ub + 3, banks[3], k - behind)

                three_units(ub, banks[0:3], KT * SET_OF[s], between)
                for k in range(KT - behind, KT):
                    fourth(ub + 3, banks[3], k)

            def prenorm(s, c, banks):
                unit(BASE[s] + c, 0, 0, banks[0])
                sum_squares(16 * s + 8)
                unit(BASE[s] + c + 1, 0, 0, banks[1], lambda: spread(stat_no(s, 0), STAT, 0, bcast_ready))

            def ffn(s):
                ub, e0 = BASE[s], FT * FFN_OF[s]
                if e0:
                    pe.wait_ge(up_scaled, e0)
                begin(s, FIRST_BANKS)
                prenorm(s, 4, (0, 1))
                unit(ub + 6, 0, 0, 2)
                pe.wait_ge(up_scaled, e0 + 2)
                unit(ub + 7, 0, 0, 3)
                with pe.Fori(2, FT // 2) as i:
                    for j in range(2):
                        pair(ub, e0, 0, 2, i, j)
                vb = ub + 2 * FT
                with pe.Fori(0, KT // 4) as i:
                    for d in range(4):
                        at = 0
                        for b, blocks in enumerate(DOWN):
                            c = vb + 3 * d + b
                            pe.wait_ge(lo_split, c + 1 + 12 * i)
                            if b == 0 and d != 1:
                                pe.wait_ge(sq_ready, 16 * s + 8 + d - 1 + 4 * i)
                            for f in range(at, at + blocks):
                                if f in (FT - 2, FT - 1) and d == 0:
                                    pe.wait_ge(hid_lo, e0 + f + 1)
                                elif f == 0 and d == 0:
                                    pe.wait_ge(hid_lo, e0 + FT - 2)
                                ins = three(ps[:, DOWN_BANK[d], :], W, block_cols(c, f - at), H, (ALL, f),
                                            f == 0, f == FT - 1)
                            at += blocks
                            ins.then_inc(unit_used, 1)
                post(s)

            def post(s):
                sum_squares(16 * s + 16)
                spread(stat_no(s, 1), STAT, 0, bcast_ready)

            def v_unit(ub, first, u):
                c = ub + first + u
                pe.wait_ge(lo_split, c + 1)
                for kk in range(2):
                    k = 2 * u + kk
                    if first == M_V0:
                        pe.wait_ge(op_lo, KT * SET_OF[1] + k + 1)
                    for tt in range(TT):
                        ins = three(ps[:, tt, :], W, (ALL, c % RING, slice(kk * T, kk * T + T)), X,
                                    (ALL, k, slice(tt * P, tt * P + P)), k == 0, k == KT - 1, swap=True)
                ins.then_inc(unit_used, 1)

            def mlstm(s):
                ub = BASE[s]
                pe.wait_ge(up_scaled, FT)
                for u in range(4):
                    v_unit(ub, M_V0, u)
                prenorm(s, M_GATE, (6, 4))
                for c in range(1, KT):
                    if c >= 2:
                        pe.wait_ge(qk_read, c - 1)
                    unit(ub + M_QK + c, 0, 0, 4 + c % 2)
                pe.wait_ge(v_kept, TT)
                for u in range(4):
                    v_unit(ub, M_V1, u)
                pe.wait_ge(gates_done, 2)
                for j, rows in enumerate((m_e[0:HEADS, 0, 2, :], m_e[0:HEADS, 1, 0, :])):
                    for st in range(TT):
                        at = (TT * j + st) * HEADS
                        ins = pe.matmul(ps[:, 6, at:at + HEADS], rows[:, st * P:(st + 1) * P],
                                        ident[0:HEADS, 0:HEADS], start=True, stop=True)
                ins.then_inc(acol_sum, 1)
                for c in range(KT):
                    if c >= 2:
                        pe.wait_ge(o_read, c - 1)
                    else:
                        pe.wait_ge(qk_read, KT - 1 + c)
                    unit(ub + M_O + c, 0, 0, 4 + c % 2)
                heads(s)

            def head_scores(h):
                if h == 0:
                    pe.wait_ge(v_kept, 2 * TT)
                    pe.wait_ge(region_zero, 3)
                    pe.wait_ge(floor_ready, 1)
                    pe.wait_ge(o_read, KT)
                else:
                    pe.wait_ge(sc_done, TT * h)
                j, par = divmod(h, 2)
                for st in range(TT):
                    bank, at = ((0, 0), (1, 0), (2, 0), (2, 256))[st]
                    ins = pe.matmul(ps[:, bank, at:at + CAUSAL[st]], m_k[par][:, j, st * P:(st + 1) * P],
                                    m_q[:, j, st * P:T], start=True, stop=True)
                ins.then_inc(s_ready, 1)
                if h >= 2:
                    pe.wait_ge(e_ready, TT * (h - 1))
                pe.matmul(ps[:, 3 + h % 2, :], ident[:, h:h + 1].to_broadcast([P, P]), m_max[:, :],
                          start=True, stop=True).then_inc(max_ready, 1)

            def heads(s):
                head_scores(0)
                for h in range(HEADS + 1):
                    if h + 1 < HEADS:
                        head_scores(h + 1)
                    if h < HEADS:
                        pe.wait_ge(sc_done, TT * (h + 1))
                        if h >= 2:
                            pe.wait_ge(og_ready, h - 1)
                        for st in range(TT):
                            ins = pe.matmul(ps[:, 5 + h % 2, P * st:T], m_v[:, st, h * P:(h + 1) * P],
                                            m_sc[:, h % 2, OFF[st]:OFF[st] + CAUSAL[st]],
                                            start=st == 0, stop=st == TT - 1)
                        ins.then_inc(num_ready, 1)
                        for t in range(TT):
                            at = TT * h + t
                            for st in range(t + 1):
                                lo = OFF[st] + (t - st) * P
                                ins = pe.matmul(ps[:, STAT, at:at + P], m_sc[:, h % 2, lo:lo + P], ones[:, :],
                                                start=st == 0, stop=st == t)
                        ins.then_inc(den_ready, 1)
                    if h >= 1:
                        g = h - 1
                        pe.wait_ge(hsq_ready, g + 1)
                        for t in range(TT):
                            at = 256 + TT * g + t
                            ins = pe.matmul(ps[:, STAT, at:at + P], sq[:, h % 2, t * P:(t + 1) * P],
                                            inv_dv[:, :], start=True, stop=True)
                        ins.then_inc(stat_sum if g == HEADS - 1 else stat_heads, 1)
                n = stat_no(s, 0) + 1
                spread(n, 3, 0, head_bcast)
                spread(n, 7, 4, head_bcast)

                def next_head(k):
                    h = k + 2
                    if h < HEADS:
                        pe.wait_ge(og_scaled, k + 1)
                        spread(n, (3, 7)[h % 2], 4 * h, head_bcast)

                out_product(s, M_OUT, next_head)

            def out_product(s, first, between=None):
                ub = BASE[s] + first
                three_units(ub, (4, 5, 6), KT * OUT_SET[s], between)
                for d in range(3, KT):
                    pe.wait_ge(sq_ready, 16 * s + 8 + d - 2)
                    unit(ub + d, 0, 0, 4 + d % 3)
                post(s)

            def window(s):
                ub = BASE[s]
                pe.wait_ge(up_scaled, FT * 3)
                begin(s, (0, 1, 2, 3))
                prenorm(s, 4, (4, 5))
                for u in range(6, W_OUT):
                    if u >= 7:
                        pe.wait_ge(b_read, u - 6)
                    unit(ub + u, 0, 0, u % 7)
                pe.wait_ge(bv_ready, 1)
                pe.wait_ge(b_read, 6)
                for n in range(NCH):
                    nk = CHUNK if n == 0 else P
                    lo = max(n - 1, 0) * CHUNK
                    pe.transpose(ps[0:nk, 4 + n // 4, (n % 4) * P:(n % 4) * P + P], ta[:, lo:lo + nk],
                                 ident[:, :]).then_inc(bw_ready, 1)
                pe.wait_ge(b_read, 8 + 4)
                chunk_scores(0)
                chunk_scores(1)
                for n in range(NCH + 1):
                    if n < NCH:
                        chunk_turn(n)
                    if n + 2 < NCH:
                        chunk_scores(n + 2)
                    if n < NCH:
                        chunk_values(n)
                pe.wait_ge(op_lo, KT * (OUT_SET[s] + 1))
                out_product(s, W_OUT)

            def chunk_scores(n):
                nk = CHUNK if n == 0 else P
                lo = max(n - 1, 0) * CHUNK
                if n >= 2:
                    pe.wait_ge(p_exp, 9 * (n - 1))
                for i in range(8):
                    g, par, jp = i // 4, i // 2 % 2, i % 2
                    j = 4 * g + 2 * jp
                    at = (i % 4) * P
                    ins = pe.matmul(ps[:, 2 * (n % 2) + i // 4, at:at + nk],
                                    b_q[:, j // 2, n, :, :].rearrange("p a t -> p (a t)"), b_k[g][par][:, lo:lo + nk],
                                    start=True, stop=True)
                ins.then_inc(bs_ready, 1)

            def chunk_turn(n):
                nk = CHUNK if n == 0 else P
                pe.wait_ge(p_ready, n + 1)
                if n == 0:
                    pe.wait_ge(bw_kept, 3)
                else:
                    pe.wait_ge(pt_act, n)
                    pe.wait_ge(pt_dve, n)
                for i in range(8):
                    ins = pe.transpose(ps[0:nk, 4 + i // 4, (i % 4) * P:(i % 4) * P + P],
                                       b_p[:, n % 2, i, 0:nk], ident[:, :])
                ins.then_inc(pt_ready, 1)

            def chunk_values(n):
                nk = CHUNK if n == 0 else P
                pe.wait_ge(pt_act, n + 1)
                pe.wait_ge(pt_dve, n + 1)
                if n >= 2:
                    pe.wait_ge(op_lo, KT * OUT_SET[4] + n - 1)
                for g in range(KV):
                    for par in range(2):
                        i = 4 * g + 2 * par
                        ins = pe.matmul(ps[par * HD:par * HD + HD, 6 + n % 2, g * 256:(g + 1) * 256],
                                        b_v[0:nk, n, g * HD:(g + 1) * HD], b_pt[0:nk, n % 2, i:i + 2, :],
                                        start=True, stop=True)
                ins.then_inc(po_ready, 1)

            pe.wait_ge(selected, 1)
            pe.wait_ge(zeroed, 6)
            for s, kind in enumerate(STAGES):
                {"ffn": ffn, "mlstm": mlstm, "window": window}[kind](s)


def stat_no(s, post):
    return 2 * s + post + (1 if 2 * s + post > 2 else 0)


def used_out(s, d):
    first = {1: M_OUT, 4: W_OUT}[s]
    return BASE[s] + first + d + 1


def tiles(np, w):
    k, n = w.shape
    return np.ascontiguousarray(
        w.reshape(k // P, P, n // P, P).transpose(2, 1, 0, 3).reshape(n // P, P, k))


def column_tiles(np, v):
    return v.reshape(-1, P).T


def kernel(x, norm_g, ffn_w_gate, ffn_w_up, ffn_w_down, a_w_in, a_conv_w, a_conv_b, a_gate_b, a_head_g,
           a_w_out, b_w_in, b_sinks, b_w_out, c_w_group, c_scale):
    import numpy as np
    import concourse.bacc as bacc
    from concourse.bass_utils import run_bass_kernel_spmd

    f32 = np.float32
    a = {k: np.asarray(v) for k, v in dict(
        x=x, g=norm_g, wg=ffn_w_gate, wu=ffn_w_up, wd=ffn_w_down, aw=a_w_in, cw=a_conv_w, cb=a_conv_b,
        gb=a_gate_b, hg=a_head_g, ao=a_w_out, bw=b_w_in, bs=b_sinks, bo=b_w_out).items()}
    x_t = np.ascontiguousarray(a["x"][0].T.reshape(KT, P, T).transpose(1, 0, 2))
    gate_up = np.stack([np.stack([tiles(np, a["wg"][l, j]), tiles(np, a["wu"][l, j])], 1).reshape(2 * FT, P, UNIT)
                        for l in range(DEPTH) for j in range(2)])
    down = np.stack([tiles(np, a["wd"][l, j]) for l in range(DEPTH) for j in range(2)])
    aw = a["aw"][0]
    qk, v, o, gate = aw[:, 0:D], aw[:, D:2 * D], aw[:, 2 * D:3 * D], aw[:, 3 * D:]
    gates = np.zeros((D, P), f32)
    gates[:, 0:HEADS] = gate[:, 0:HEADS]
    gates[:, 32:32 + HEADS] = gate[:, HEADS:]
    vt = v.reshape(KT // 2, 2, P, 2, T).transpose(3, 0, 2, 1, 4).reshape(KT, P, UNIT)
    mlstm_w = np.concatenate([vt[0:4], tiles(np, gates), tiles(np, qk), vt[4:8], tiles(np, o),
                              tiles(np, a["ao"][0])])
    window_w = np.concatenate([tiles(np, a["bw"][0]), tiles(np, a["bo"][0])])
    gate_b = np.zeros((P, 1), f32)
    gate_b[0:HEADS, 0] = a["gb"][0, 0:HEADS]
    gate_b[32:32 + HEADS, 0] = a["gb"][0, HEADS:]
    conv_w = a["cw"][0].T.reshape(KT, P, TAPS).transpose(1, 0, 2).reshape(P, KT * TAPS)
    sink = a["bs"][0].reshape(KV, 2, 2, 2).transpose(2, 0, 3, 1).reshape(2, 8)
    consts = np.ascontiguousarray(np.concatenate(
        [column_tiles(np, a["g"].reshape(-1)), column_tiles(np, a["hg"][0]), conv_w, column_tiles(np, a["cb"][0]),
         gate_b, np.repeat(sink, HD, axis=0)], axis=1))

    nc = bacc.Bacc("TRN2", target_bir_lowering=False, num_devices=1)
    arrays, args = {}, []
    for name, arr in (("x_t", x_t), ("consts_in", consts), ("gate_up", gate_up), ("down", down),
                      ("mlstm_w", mlstm_w), ("window_w", window_w)):
        arrays[name] = np.ascontiguousarray(arr)
        args.append(nc.dram_tensor(name, arr.shape, mybir.dt.from_np(arr.dtype), kind="ExternalInput").ap())
    args.append(nc.dram_tensor("out_t", (P, KT, T), F32, kind="ExternalOutput").ap())
    build(nc, *args)
    r = run_bass_kernel_spmd(nc, [arrays], core_ids=[0])
    out = r.results[0]["out_t"]
    return np.ascontiguousarray(out.transpose(2, 1, 0).reshape(1, T, D))
```

```python
from contextlib import ExitStack

import concourse.bass as bass
from concourse import mybir

F32 = mybir.dt.float32
F32R = mybir.dt.float32r
ALU = mybir.AluOpType
ACT = mybir.ActivationFunctionType
AX_X = mybir.AxisListType.X

P = 128
T = 512
D = 1024
KT = D // P
TT = T // P
HALF = (slice(0, T // 2), slice(T // 2, T))
F = 2816
FT = F // P
EPS = 1e-6
CHUNK = 64
NCH = T // CHUNK
DEPTH = 2
NORMS = 6

HEADS = 8
DQK = 64
TAPS = 4
CAP = 15.0

KV = 2
HD = 64

RING = 4
UNIT = 1024
DOWN = (8, 8, 6)

STAGES = ("ffn", "mlstm", "ffn", "ffn", "window", "ffn")
FFN_UNITS = 2 * FT + 3 * KT
M_V0, M_GATE, M_QK, M_V1, M_O, M_OUT, M_UNITS = 0, 4, 5, 13, 17, 25, 33
W_Q, W_K, W_V, W_OUT, W_UNITS = 0, 8, 9, 10, 18
UNITS = {"ffn": FFN_UNITS, "mlstm": M_UNITS, "window": W_UNITS}
BASE = [sum(UNITS[k] for k in STAGES[:s]) for s in range(len(STAGES) + 1)]
FFN_OF = {0: 0, 2: 1, 3: 2, 5: 3}
OUT_SET = {1: 1, 4: 2}
HALVED = {"ffn": (KT - 1,), "mlstm": (KT - 3, KT - 2, KT - 1), "window": (KT - 3, KT - 2, KT - 1)}

C_GAIN = 0
C_HEADG = C_GAIN + DEPTH * NORMS * KT
C_CONVW = C_HEADG + HEADS
C_CONVB = C_CONVW + KT * TAPS
C_GATEB = C_CONVB + KT
C_SINK = C_GATEB + 1
C_ALL = C_SINK + 8

STAT = 7
STAT_B = 1
FIRST_BANKS = (4, 5, 6, 3)
DOWN_BANK = (4, 5, 4, 6)
SECOND_BANK = (0, 2, 3)
V_BANKS = (4, 5, 2, 3)
W_BANKS = FIRST_BANKS + (0, 1, 2, 4, 5, 6)

BIG = 3e38


def out_bank(s, d):
    if STAGES[s] == "ffn":
        return DOWN_BANK[d % 4]
    return d if d < 3 else 4 + d % 3


def o_bank(c):
    return (0 if c < 2 else 4) + c % 2


def gain_col(stage, post, k):
    layer, j = divmod(stage, 3)
    return C_GAIN + (layer * NORMS + 2 * j + post) * KT + k


def build(nc, x_t, consts_d, gate_up, down, mlstm_w, window_w, out_t):
    with ExitStack() as ctx:
        def sb(name, shape, dt=F32, to=ctx):
            return to.enter_context(nc.sbuf_tensor(name, shape, dt))

        def sem(name):
            return ctx.enter_context(nc.semaphore(name))

        x = sb("x", [P, KT, T])
        raw = sb("raw", [P, RING, UNIT])
        w_hi = sb("w_hi", [P, RING, UNIT], F32R)
        w_lo = sb("w_lo", [P, RING, UNIT], F32R)
        consts = sb("consts", [P, C_ALL])
        half_gain = sb("half_gain", [P, C_CONVW])
        gate_b15 = sb("gate_b15", [P, 1])
        table_call = sb("table_call", [P, 1])
        ident = sb("ident", [P, P])
        ident_hi = sb("ident_hi", [P, P], F32R)
        ones = sb("ones", [P, P])
        inv_d = sb("inv_d", [P, P])
        inv_dv = sb("inv_dv", [P, P])
        causal = sb("causal", [P, P])
        zeros = sb("zeros", [HEADS, T])
        rs = sb("rs", [P, T])
        acc = sb("acc", [P, T])
        sq = sb("sq", [P, 2, T])
        ms = sb("ms", [P, 4 * HEADS])
        root = sb("root", [P, 4 * HEADS])
        rcol = sb("rcol", [P, 4 * HEADS])
        ta = sb("ta", [P, T])
        tb = sb("tb", [P, T])
        tc = sb("tc", [P, T])
        x_hi = sb("x_hi", [P, KT, T], F32R)
        with ExitStack() as own:
            x_lo = sb("x_lo", [P, KT, T], F32R, own)
        with ExitStack() as own:
            y_ffn = sb("y_ffn", [P, KT, T], F32, own)
        ctx.enter_context(nc.sbuf_tensor("x_lo_room", [P, KT, T], F32))
        with ExitStack() as own:
            h_hi = sb("h_hi", [P, FT, T], F32R, own)
            h_lo = sb("h_lo", [P, FT, T], F32R, own)
        CAUSAL = [T - P * st for st in range(TT)]
        OFF = [sum(CAUSAL[:st]) for st in range(TT)]
        with ExitStack() as own:
            m_q = sb("m_q", [P, KT // 2, T], F32, own)
            m_k = [sb(f"m_k{par}", [P, KT // 2, T], F32, own) for par in range(2)]
            m_o = sb("m_o", [P, KT, T], F32, own)
            m_v = sb("m_v", [P, TT, D], F32, own)
            m_e = sb("m_e", [P, 2, TT, T], F32, own)
            m_sc = sb("m_sc", [P, 2, sum(CAUSAL)], F32, own)
            m_max = sb("m_max", [P, T], F32, own)
            m_max_hi = sb("m_max_hi", [P, T], F32R, own)
            m_max_lo = sb("m_max_lo", [P, T], F32R, own)
        with ExitStack() as own:
            y_mix = sb("y_mix", [P, KT, T], F32, own)
        with ExitStack() as own:
            b_q = sb("b_q", [P, KT // 2, NCH, 2, CHUNK], F32, own)
            b_k = [[sb(f"b_k{g}{par}", [P, T], F32, own) for par in range(2)] for g in range(KV)]
            b_v = sb("b_v", [P, NCH, P], F32, own)
            b_p = sb("b_p", [P, 2, 8, P], F32, own)
            b_pt = sb("b_pt", [P, 2, 8, P], F32, own)
        ctx.enter_context(nc.sbuf_tensor("region", [P, 2 * FT, T], F32))
        u_conv = sb("u_conv", [P, TAPS - 1 + T])
        acol = sb("acol", [P, TT * HEADS])
        floor = sb("floor", [P, HEADS, TT])
        dmag = sb("dmag", [P, 4 * HEADS])
        dneg = sb("dneg", [P, 4 * HEADS])
        dinv = sb("dinv", [P, 4 * HEADS])
        low = sb("low", [P, 2, 8])
        nmx = sb("nmx", [P, 2, 8])
        smx = sb("smx", [P, 2, 8])
        esk = sb("esk", [P, 2, 8])
        sm = sb("sm", [P, 2, 8])
        den = sb("den", [P, 2, 8])
        rden = sb("rden", [P, 2, 8])

        ps = ctx.enter_context(nc.psum_tensor("ps", [P, 8, T], F32))

        consts_landed = sem("consts_landed")
        x_landed = [sem(f"x_landed{k}") for k in range(KT)]
        start_landed = [sem(f"start_landed{k}") for k in range(KT + 1)]
        start_hi = sem("start_hi")
        start_lo = sem("start_lo")
        raw_landed = [sem(f"raw_landed{r}") for r in range(RING)]
        out_sent = sem("out_sent")
        hi_split = sem("hi_split")
        lo_split = sem("lo_split")
        unit_used = sem("unit_used")
        zeroed = sem("zeroed")
        selected = sem("selected")
        scaled_consts = sem("scaled_consts")
        op_hi = sem("op_hi")
        op_lo = sem("op_lo")
        in_hi = [sem(f"in_hi{h}") for h in range(2)]
        in_lo = [sem(f"in_lo{h}") for h in range(2)]
        y_scaled = [sem(f"y_scaled{h}") for h in range(2)]
        x_new = [sem(f"x_new{h}") for h in range(2)]
        first_done = sem("first_done")
        first_sq = sem("first_sq")
        first_y = sem("first_y")
        first_acc = sem("first_acc")
        first_sum = sem("first_sum")
        first_ms = sem("first_ms")
        first_root = sem("first_root")
        first_rcol = sem("first_rcol")
        first_bcast = sem("first_bcast")
        sq_ready = sem("sq_ready")
        acc_done = sem("acc_done")
        acc_cleared = sem("acc_cleared")
        stat_sum = sem("stat_sum")
        ms_ready = sem("ms_ready")
        root_ready = sem("root_ready")
        rcol_ready = sem("rcol_ready")
        bcast_ready = sem("bcast_ready")
        rs_ready = sem("rs_ready")
        y_ready = sem("y_ready")
        gate_scaled = sem("gate_scaled")
        up_scaled = sem("up_scaled")
        silu_ready = sem("silu_ready")
        hid_ready = sem("hid_ready")
        hid_hi = sem("hid_hi")
        hid_lo = sem("hid_lo")
        region_zero = sem("region_zero")
        vchain = sem("vchain")
        achain = sem("achain")
        v_kept = sem("v_kept")
        gate_z = sem("gate_z")
        gate_tanh = sem("gate_tanh")
        gate_l = sem("gate_l")
        gates_done = sem("gates_done")
        ident_ready = sem("ident_ready")
        max_hi = sem("max_hi")
        max_lo = sem("max_lo")
        acol_sum = sem("acol_sum")
        acol_ready = sem("acol_ready")
        qk_read = sem("qk_read")
        conv_ready = sem("conv_ready")
        qk_silu = sem("qk_silu")
        o_read = sem("o_read")
        o_tanh = sem("o_tanh")
        s_ready = sem("s_ready")
        max_ready = sem("max_ready")
        e_ready = sem("e_ready")
        e_masked = sem("e_masked")
        floor_ready = sem("floor_ready")
        sc_done = sem("sc_done")
        tot_done = sem("tot_done")
        num_ready = sem("num_ready")
        den_ready = sem("den_ready")
        hsq_ready = sem("hsq_ready")
        stat_heads = sem("stat_heads")
        og_ready = sem("og_ready")
        heads_read = sem("heads_read")
        heads_ms = sem("heads_ms")
        heads_root = sem("heads_root")
        heads_rcol = sem("heads_rcol")
        head_bcast = sem("head_bcast")
        og_scaled = sem("og_scaled")
        b_read = sem("b_read")
        bv_ready = sem("bv_ready")
        bw_ready = sem("bw_ready")
        bw_kept = sem("bw_kept")
        bs_ready = sem("bs_ready")
        nmx_ready = sem("nmx_ready")
        smx_ready = sem("smx_ready")
        p_exp = sem("p_exp")
        p_ready = sem("p_ready")
        pt_ready = sem("pt_ready")
        pt_act = sem("pt_act")
        pt_dve = sem("pt_dve")
        po_ready = sem("po_ready")

        block = ctx.enter_context(nc.Block())

        @block.sync
        def _(sp):
            for k in range(KT):
                sp.dma_start(x[:, k, :], x_t[:, k, :]).then_inc(x_landed[k], 16)
                cols = slice(k * P, (k + 1) * P)
                sp.dma_start(raw[:, 0:3, cols], gate_up[0, 0:3, :, cols].rearrange("u p c -> p u c")).then_inc(
                    start_landed[k], 16)
                if k == 0:
                    sp.dma_start(consts[:, :], consts_d).then_inc(consts_landed, 16)
            sp.dma_start(raw[:, 3, :], gate_up[0, 3]).then_inc(start_landed[KT], 16)

            def load_unit(c, m, i, src):
                slot = c % RING
                sp.wait_ge(lo_split, c - RING + 1 + m * i)
                sp.dma_start(raw[:, slot, 0:src.shape[-1]], src).then_inc(raw_landed[slot], 16)

            for s, kind in enumerate(STAGES):
                ub = BASE[s]
                if kind == "ffn":
                    n = FFN_OF[s]
                    if s:
                        for u in range(4):
                            load_unit(ub + u, 0, 0, gate_up[n, u])
                    else:
                        sp.wait_ge(lo_split, 3)
                    with sp.Fori(1, FT // 2) as i:
                        for u in range(4):
                            load_unit(ub + u, 4, i, gate_up[n, bass.ds(4 * i + u, 1)].rearrange("a p c -> (a p) c"))
                    with sp.Fori(0, KT // 4) as i:
                        for d in range(4):
                            tile = down[n, bass.ds(4 * i + d, 1)].rearrange("a p c -> (a p) c")
                            at = 0
                            for b, blocks in enumerate(DOWN):
                                load_unit(ub + 2 * FT + 3 * d + b, 12, i, tile[:, at:at + blocks * P])
                                at += blocks * P
                else:
                    src = mlstm_w if kind == "mlstm" else window_w
                    for u in range(UNITS[kind]):
                        load_unit(ub + u, 0, 0, src[u])
            last = len(STAGES) - 1
            for h in range(2):
                for k in range(KT):
                    sp.wait_ge(x_new[h], KT * last + k + 1)
                    sp.dma_start(out_t[:, k, HALF[h]], x[:, k, HALF[h]]).then_inc(out_sent, 16)
            sp.wait_ge(out_sent, 16 * 2 * KT)

        @block.gpsimd
        def _(pool):
            pool.memset(ident[:, :], 0.0).then_inc(zeroed, 1)
            pool.wait_ge(zeroed, 1)
            pool.affine_select(out=ident[:, :], in_=ident[:, :], compare_op=ALU.not_equal, fill=1.0, base=0,
                               pattern=[[-1, P]], channel_multiplier=1).then_inc(selected, 1)
            pool.memset(ones[:, :], 1.0).then_inc(zeroed, 1)
            pool.memset(inv_d[:, :], 1.0 / D).then_inc(zeroed, 1)
            pool.memset(inv_dv[:, :], 1.0 / P).then_inc(zeroed, 1)
            pool.memset(zeros[:, :], 0.0).then_inc(zeroed, 1)
            pool.memset(u_conv[:, 0:TAPS - 1], 0.0).then_inc(zeroed, 1)
            pool.wait_ge(zeroed, 2)
            pool.affine_select(out=causal[:, :], in_=ones[:, :], compare_op=ALU.is_ge, fill=0.0, base=0,
                               pattern=[[1, P]], channel_multiplier=-1).then_inc(selected, 1)

            pool.wait_ge(selected, 2)
            pool.wait_ge(unit_used, BASE[1])
            pool.memset(m_k[0][HD:P, :, :], 0.0).then_inc(region_zero, 1)
            pool.wait_ge(region_zero, 1)
            pool.memset(m_k[1][0:HD, :, :], 0.0).then_inc(region_zero, 1)
            pool.wait_ge(region_zero, 2)
            pool.memset(m_max[:, :], 0.0).then_inc(region_zero, 1)
            pool.wait_ge(unit_used, BASE[4])
            for g in range(KV):
                pool.wait_ge(region_zero, 3 + 2 * g)
                pool.memset(b_k[g][0][HD:P, :], 0.0).then_inc(region_zero, 1)
                pool.wait_ge(region_zero, 3 + 2 * g + 1)
                pool.memset(b_k[g][1][0:HD, :], 0.0).then_inc(region_zero, 1)

        @block.scalar
        def _(act):
            steps = [0]

            def link(ins):
                steps[0] += 1
                ins.then_inc(achain, 1)
                act.wait_ge(achain, steps[0])

            def split_hi(c, m=0, i=0, cols=UNIT):
                slot, u = c % RING, c + m * i
                if isinstance(u, int) and u == RING - 1:
                    act.wait_ge(start_landed[KT], 16)
                else:
                    act.wait_ge(raw_landed[slot], 16 * (c // RING) + 16 * (m // RING) * i)
                    act.wait_ge(unit_used, u - RING + 1)
                act.activation(w_hi[:, slot, 0:cols], raw[:, slot, 0:cols], ACT.Copy).then_inc(hi_split, 1)

            def square(q, m, i, src):
                if q >= 2:
                    act.wait_ge(acc_done, q - 1 + m * i)
                act.activation(sq[:, q % 2, :], src, ACT.Square).then_inc(sq_ready, 1)

            def input_hi(s, h, k):
                act.wait_ge(x_new[h], KT * (s - 1) + k + 1)
                g = gain_col(s, 0, k)
                act.activation(x_hi[:, k, HALF[h]], x[:, k, HALF[h]], ACT.Copy,
                               scale=consts[:, g:g + 1]).then_inc(in_hi[h], 1)

            def input_tiles(s):
                for k in range(KT):
                    if s == 0:
                        act.wait_ge(start_landed[k], 16)
                        cols = slice(k * P, (k + 1) * P)
                        act.activation(w_hi[:, 0:3, cols], raw[:, 0:3, cols], ACT.Copy).then_inc(
                            *((start_hi, 1) if k < KT - 3 else (hi_split, 1)))
                        act.wait_ge(x_landed[k], 16)
                        if k == 0:
                            act.wait_ge(consts_landed, 16)
                        g = gain_col(s, 0, k)
                        act.activation(x_hi[:, k, :], x[:, k, :], ACT.Copy,
                                       scale=consts[:, g:g + 1]).then_inc(op_hi, 1)
                    else:
                        input_hi(s, 1, k)
                    if k < 2:
                        input_square(s, k)
                if s == 0:
                    split_hi(RING - 1)

            def input_square(s, k):
                square(16 * s + k, 0, 0, x[:, k, :])

            def input_squares(s):
                split_hi(BASE[s] + 4)
                for k in range(2, KT):
                    input_square(s, k)
                split_hi(BASE[s] + 5)

            def sqrt_stat(n):
                act.wait_ge(ms_ready, n + 1)
                act.activation(root[:, 0:TT], ms[:, 0:TT], ACT.Sqrt).then_inc(root_ready, 1)

            def keep_rs(s):
                act.wait_ge(bcast_ready, 2 * s + 1)
                act.activation(rs[:, :], ps[:, STAT, :], ACT.Copy).then_inc(rs_ready, 1)

            def output_tile(s, c, m, i, bank, gain, y, used):
                act.wait_ge(unit_used, used)
                d = c + m * i
                col = gain_col(s, 1, 0) + d
                dst = y[:, bass.ds(d, 1), :].rearrange("p a t -> p (a t)")
                act.activation(dst, ps[:, bank, :], ACT.Copy, scale=gain[:, bass.ds(col, 1)]).then_inc(y_ready, 1)
                square(16 * s + 8 + c, m, i, ps[:, bank, :])

            def half_tile(s, n, h, gain, y, used):
                d = HALVED[STAGES[s]][n]
                if h == 0:
                    act.wait_ge(first_done, used)
                    act.wait_ge(acc_done, 16 * s + 8 + d - 1 - max(n - 1, 0))
                else:
                    act.wait_ge(unit_used, used)
                    act.wait_ge(acc_done, 16 * s + 8 + d - 1)
                bank = SECOND_BANK[n] if h else out_bank(s, d)
                col = gain_col(s, 1, d)
                src = ps[:, bank, HALF[h]]
                q = 16 * s + 8 + d
                if h == 0 and n >= 2:
                    act.wait_ge(first_acc, used - 2)
                act.activation(sq[:, q % 2, HALF[h]], src, ACT.Square).then_inc(sq_ready if h else first_sq, 1)
                act.activation(y[:, d, HALF[h]], src, ACT.Copy,
                               scale=gain[:, col:col + 1]).then_inc(y_ready if h else first_y, 1)

            def tail(s, gain, y):
                tiles_here = HALVED[STAGES[s]]
                nb, last = BASE[s + 1], s + 1 == len(STAGES)
                before = first_tiles(s)
                act.activation(table_call[:, :], ones[:, 0:1], ACT.Sqrt)
                for n in range(len(tiles_here)):
                    half_tile(s, n, 0, gain, y, before + n + 1)
                act.wait_ge(first_ms, s + 1)
                act.activation(root[:, 0:2], ms[:, 0:2], ACT.Sqrt).then_inc(first_root, 1)
                if not last:
                    split_hi(nb + 1)
                    for k in range(4):
                        input_hi(s + 1, 0, k)
                for n in range(len(tiles_here)):
                    half_tile(s, n, 1, gain, y, nb - len(tiles_here) + n + 1)
                if not last:
                    split_hi(nb + 2)
                    input_hi(s + 1, 0, 4)
                act.wait_ge(ms_ready, stat_no(s, 1) + 1)
                act.activation(root[:, 2:4], ms[:, 2:4], ACT.Sqrt).then_inc(root_ready, 1)
                if not last:
                    split_hi(nb + 3)
                    for k in range(5, KT):
                        input_hi(s + 1, 0, k)

            def hidden(e, c, m, i):
                act.wait_ge(gate_scaled, e + m * i + 1)
                act.activation(tc[:, :], ta[:, :], ACT.Silu).then_inc(silu_ready, 1)
                act.wait_ge(hid_ready, e + m * i + 1)
                dst = h_hi[:, bass.ds(c + m * i, 1), :].rearrange("p a t -> p (a t)")
                act.activation(dst, tb[:, :], ACT.Copy).then_inc(hid_hi, 1)

            def ffn(s):
                ub, e0 = BASE[s], FT * FFN_OF[s]
                input_tiles(s)
                input_squares(s)
                split_hi(ub + 6)
                sqrt_stat(stat_no(s, 0))
                split_hi(ub + 7)
                keep_rs(s)
                for c in range(4):
                    if c == 3:
                        split_hi(ub + 8)
                        split_hi(ub + 9)
                    hidden(e0 + c, c, 0, 0)
                with act.Fori(2, FT // 2) as i:
                    for j in range(2):
                        split_hi(ub + 2 * j + 2, 4, i)
                        split_hi(ub + 2 * j + 3, 4, i)
                        hidden(e0 + j, j, 2, i)
                vb = ub + 2 * FT
                split_hi(vb + 2, 0, 0, DOWN[2] * P)

                def output_tiles(i, n):
                    for d in range(n):
                        for b in range(3):
                            split_hi(vb + 3 * d + b + 3, 12, i, DOWN[b] * P)
                        output_tile(s, d, 4, i, DOWN_BANK[d], half_gain, y_ffn, vb + 3 * d + 3 + 12 * i)

                with act.Fori(0, KT // 4 - 1) as i:
                    output_tiles(i, 4)
                output_tiles(KT // 4 - 1, 3)
                if s + 1 < len(STAGES):
                    split_hi(BASE[s + 1])
                tail(s, half_gain, y_ffn)

            def mlstm(s):
                ub = BASE[s]
                input_tiles(s)
                input_squares(s)
                for u in range(M_UNITS - 2):
                    if u == M_GATE:
                        split_hi(ub + M_GATE + 2)
                        sqrt_stat(stat_no(s, 0))
                        split_hi(ub + M_GATE + 3)
                        keep_rs(s)
                    if M_GATE < u:
                        split_hi(ub + u + 3)
                    if u == M_GATE:
                        act.wait_ge(gate_z, 1)
                        act.activation(tc[0:40, :], m_e[0:40, 1, 1, :], ACT.Tanh, bias=gate_b15[0:40, :],
                                       scale=1.0 / CAP).then_inc(gate_tanh, 1)
                        act.wait_ge(gate_tanh, 1)
                        link(act.activation(m_e[0:HEADS, 1, 2, :], tc[32:40, :], ACT.Exp, scale=-CAP))
                        act.activation(m_e[0:HEADS, 0, 1, :], m_e[0:HEADS, 1, 2, :], ACT.Ln,
                                       bias=ones[0:HEADS, 0:1]).then_inc(gate_l, 1)
                    if M_QK <= u < M_QK + TT:
                        keep_v(0, u - M_QK)
                    if M_QK < u <= M_QK + KT:
                        c = u - M_QK - 1
                        act.wait_ge(conv_ready, c + 1)
                        src = (ta, tb)[c % 2]
                        if c < KT // 2:
                            act.activation(m_q[:, c, :], src[:, :], ACT.Silu).then_inc(qk_silu, 1)
                        else:
                            act.activation(m_k[0][0:HD, c - KT // 2, :], src[0:HD, :], ACT.Silu)
                            act.activation(m_k[1][HD:P, c - KT // 2, :], src[HD:P, :],
                                           ACT.Silu).then_inc(qk_silu, 1)
                    if u == M_V1 + 1:
                        act.wait_ge(gates_done, 1)
                        act.activation(m_max_hi[:, :], m_max[:, :], ACT.Copy).then_inc(max_hi, 1)
                    if u == M_V1 + 3:
                        for tt in range(TT):
                            keep_v(1, tt)
                        act.wait_ge(acol_ready, 1)
                        act.activation(floor[:, :, :].rearrange("p h t -> p t h"),
                                       ps[:, 6, TT * HEADS:2 * TT * HEADS].rearrange("p (t h) -> p t h", t=TT),
                                       ACT.Exp).then_inc(floor_ready, 1)
                    if u == M_O + KT - 1:
                        head_exp(0)
                    if M_O <= u < M_O + KT:
                        c = u - M_O
                        act.wait_ge(o_read, c + 1)
                        act.activation(m_o[:, c, :], (ta, tb)[c % 2][:, :], ACT.Tanh, scale=0.5).then_inc(o_tanh, 1)
                    if u == M_OUT - 1:
                        heads(s)
                    if M_OUT <= u:
                        d = u - M_OUT
                        if d < HALVED["mlstm"][0]:
                            output_tile(s, d, 0, 0, out_bank(s, d), consts, y_mix, used_out(s, d))
                tail(s, consts, y_mix)

            def keep_v(half, tt):
                act.wait_ge(unit_used, BASE[1] + (M_V0 if half == 0 else M_V1) + 4)
                act.wait_ge(rcol_ready, stat_no(1, 0) + 1)
                act.activation(m_v[:, tt, half * T:half * T + T], ps[:, V_BANKS[tt], :], ACT.Copy,
                               scale=rcol[:, tt:tt + 1]).then_inc(v_kept, 1)

            def head_exp(h):
                act.wait_ge(acol_ready, 1)
                act.wait_ge(gates_done, 2)
                act.wait_ge(max_ready, h + 1)
                if h >= 2:
                    act.wait_ge(sc_done, TT * (h - 1))
                for st in range(TT):
                    act.activation(m_e[:, h % 2, st, 0:CAUSAL[st]], ps[:, 3 + h % 2, P * st:T], ACT.Exp,
                                   bias=acol[:, st * HEADS + h:st * HEADS + h + 1]).then_inc(e_ready, 1)

            def heads(s):
                for h in range(1, HEADS + 1):
                    if h < HEADS:
                        head_exp(h)
                    if h >= 1:
                        act.wait_ge(num_ready, h)
                        if h >= 3:
                            act.wait_ge(stat_heads, h - 2)
                        act.activation(sq[:, h % 2, :], ps[:, 5 + (h - 1) % 2, :], ACT.Square).then_inc(hsq_ready, 1)
                    if h == 6:
                        heads_sqrt(0)
                for h in range(HEADS):
                    if h == 1:
                        heads_sqrt(1)
                    act.wait_ge(og_scaled, h + 1)
                    act.activation(x_hi[:, h, :], m_o[:, h, :], ACT.Copy,
                                   scale=half_gain[:, C_HEADG + h:C_HEADG + h + 1]).then_inc(op_hi, 1)

            def heads_sqrt(g):
                cols = slice(TT * 4 * g, TT * 4 * (g + 1))
                act.wait_ge(heads_ms, g + 1)
                act.activation(root[:, cols], ms[:, cols], ACT.Sqrt).then_inc(heads_root, 1)

            def window(s):
                ub = BASE[s]
                input_tiles(s)
                input_squares(s)
                split_hi(ub + 6)
                sqrt_stat(stat_no(s, 0))
                split_hi(ub + 7)
                keep_rs(s)
                for u in range(W_UNITS - 2):
                    if u > 4:
                        split_hi(ub + u + 3)
                    if u == W_V:
                        chunk_exp(0)
                        act.wait_ge(bw_ready, 8)
                        act.activation(b_v[0:CHUNK, 0, :], ps[0:CHUNK, 4, 0:P], ACT.Copy).then_inc(bw_kept, 1)
                        act.activation(b_v[:, 1:4, :], ps[:, 4, P:T].rearrange("p (a b) -> p a b", a=3),
                                       ACT.Copy).then_inc(bw_kept, 1)
                        act.activation(b_v[:, 4:8, :], ps[:, 5, :].rearrange("p (a b) -> p a b", a=4),
                                       ACT.Copy).then_inc(bw_kept, 1)
                        chunk_exp(1)
                        for n in range(NCH):
                            chunk_turn(n)
                            if n + 2 < NCH:
                                chunk_exp(n + 2)
                            chunk_round(n)
                    if W_OUT <= u:
                        d = u - W_OUT
                        if d < HALVED["mlstm"][0]:
                            output_tile(s, d, 0, 0, out_bank(s, d), consts, y_mix, used_out(s, d))
                tail(s, consts, y_mix)

            def chunk_exp(n):
                keys = slice(0, CHUNK if n == 0 else P)
                act.wait_ge(nmx_ready, n + 1)
                if n >= 2:
                    act.wait_ge(pt_ready, n - 1)
                for i in range(8):
                    act.activation(b_p[:, n % 2, i, keys], ps[:, 2 * (n % 2) + i // 4, :].rearrange(
                        "p (a b) -> p a b", a=4)[:, i % 4, keys], ACT.Exp, bias=nmx[:, n % 2, i:i + 1], scale=-1.0,
                        accum_out=sm[:, n % 2, i:i + 1]).then_inc(p_exp, 1)
                act.wait_ge(smx_ready, n + 1)
                act.activation(esk[:, n % 2, :], smx[:, n % 2, :], ACT.Exp).then_inc(p_exp, 1)

            def chunk_turn(n):
                rows = slice(0, CHUNK if n == 0 else P)
                act.wait_ge(pt_ready, n + 1)
                if n >= 2:
                    act.wait_ge(po_ready, n - 1)
                act.activation(b_pt[rows, n % 2, 0:4, :], ps[rows, 4, :].rearrange("p (a b) -> p a b", a=4),
                               ACT.Copy).then_inc(pt_act, 1)

            def chunk_round(n):
                act.wait_ge(po_ready, n + 1)
                act.activation(x_hi[:, :, n * CHUNK:(n + 1) * CHUNK],
                               ps[:, 6 + n % 2, :].rearrange("p (a b) -> p a b", a=8), ACT.Copy).then_inc(op_hi, 1)

            act.wait_ge(selected, 1)
            act.activation(ident_hi[:, :], ident[:, :], ACT.Copy).then_inc(ident_ready, 1)
            for s, kind in enumerate(STAGES):
                {"ffn": ffn, "mlstm": mlstm, "window": window}[kind](s)

        @block.vector
        def _(dve):
            steps = [0]

            def link(ins):
                steps[0] += 1
                ins.then_inc(vchain, 1)
                dve.wait_ge(vchain, steps[0])

            def split_lo(c, m=0, i=0, cols=UNIT):
                slot, u = c % RING, c + m * i
                dve.wait_ge(hi_split, u + 1)
                dve.tensor_tensor(w_lo[:, slot, 0:cols], raw[:, slot, 0:cols], w_hi[:, slot, 0:cols].bitcast(F32),
                                  ALU.subtract).then_inc(lo_split, 1)

            def add_square(q, m, i, s, cols=slice(0, T)):
                dve.wait_ge(acc_cleared, s + 1)
                dve.wait_ge(acc_done, q + m * i)
                dve.wait_ge(sq_ready, q + m * i + 1)
                dve.tensor_tensor(acc[:, cols], acc[:, cols], sq[:, q % 2, cols], ALU.add).then_inc(acc_done, 1)

            def start_lo_tile(k):
                cols = slice(k * P, (k + 1) * P)
                if k < KT - 3:
                    dve.wait_ge(start_hi, k + 1)
                else:
                    dve.wait_ge(hi_split, k - (KT - 3) + 1)
                dve.tensor_tensor(w_lo[:, 0:3, cols], raw[:, 0:3, cols], w_hi[:, 0:3, cols].bitcast(F32),
                                  ALU.subtract).then_inc(*((start_lo, 1) if k < KT - 3 else (lo_split, 1)))
                dve.wait_ge(op_hi, k + 1)
                input_lo(0, slice(0, T), k, op_lo)

            def input_lo(s, cols, k, done):
                g = gain_col(s, 0, k)
                dve.scalar_tensor_tensor(out=x_lo[:, k, cols], in0=x[:, k, cols], scalar=consts[:, g:g + 1],
                                         in1=x_hi[:, k, cols].bitcast(F32), op0=ALU.mult,
                                         op1=ALU.subtract).then_inc(done, 1)

            def scale_y(s, h, k):
                y = y_of(s)
                if h == 0:
                    dve.wait_ge(first_bcast, s + 1)
                else:
                    dve.wait_ge(bcast_ready, 2 * s + 2)
                here = HALVED[STAGES[s]]
                if h == 0 and k >= here[0]:
                    dve.wait_ge(first_y, first_tiles(s) + k - here[0] + 1)
                else:
                    dve.wait_ge(y_ready, KT * s + k + 1)
                dve.tensor_tensor(y[:, k, HALF[h]], y[:, k, HALF[h]], ps[:, STAT_B if h else STAT, HALF[h]],
                                  ALU.mult).then_inc(y_scaled[h], 1)

            def add_y(s, h, k):
                y = y_of(s)
                dve.wait_ge(y_scaled[h], KT * s + k + 1)
                dve.tensor_tensor(x[:, k, HALF[h]], x[:, k, HALF[h]], y[:, k, HALF[h]],
                                  ALU.add).then_inc(x_new[h], 1)

            def residual(s, h, between=None):
                last = s + 1 == len(STAGES)
                scale_y(s, h, 0)
                for k in range(KT + 1):
                    if between:
                        between(k)
                    if k + 1 < KT:
                        scale_y(s, h, k + 1)
                    if k < KT:
                        add_y(s, h, k)
                    if k >= 1 and not last:
                        dve.wait_ge(in_hi[h], KT * s + k)
                        input_lo(s + 1, HALF[h], k - 1, in_lo[h])

            def input_tiles(s):
                if s:
                    residual(s - 1, 1)
                else:
                    for k in range(KT):
                        start_lo_tile(k)
                    split_lo(RING - 1)

            def tail(s):
                tiles_here = HALVED[STAGES[s]]
                last = s + 1 == len(STAGES)
                before = first_tiles(s)
                q = 16 * s + 8 + tiles_here[0]
                for n in range(len(tiles_here)):
                    dve.wait_ge(acc_done, q)
                    if before + n:
                        dve.wait_ge(first_acc, before + n)
                    dve.wait_ge(first_sq, before + n + 1)
                    dve.tensor_tensor(acc[:, HALF[0]], acc[:, HALF[0]], sq[:, (q + n) % 2, HALF[0]],
                                      ALU.add).then_inc(first_acc, 1)
                dve.wait_ge(first_sum, s + 1)
                dve.tensor_scalar(ms[:, 0:2], ps[:, STAT, 0:2], EPS, None, ALU.add).then_inc(first_ms, 1)
                dve.wait_ge(first_root, s + 1)
                dve.reciprocal(rcol[:, 0:2], root[:, 0:2]).then_inc(first_rcol, 1)
                nb = BASE[s + 1]

                def between(k):
                    if not last and k == 2:
                        split_lo(nb + 1)
                    if k == 4:
                        for n in range(len(tiles_here)):
                            add_square(q + n, 0, 0, s, HALF[1])
                    if k == 5:
                        dve.wait_ge(stat_sum, stat_no(s, 1) + 1)
                        dve.tensor_scalar(ms[:, 2:4], ps[:, STAT_B, 2:4], EPS, None, ALU.add).then_inc(ms_ready, 1)
                    if not last and k == 5:
                        split_lo(nb + 2)
                    if k == 6:
                        dve.wait_ge(root_ready, stat_no(s, 1) + 1)
                        dve.reciprocal(rcol[:, 2:4], root[:, 2:4]).then_inc(rcol_ready, 1)
                    if not last and k == 6:
                        split_lo(nb + 3)

                residual(s, 0, between)

            def input_squares(s):
                for k in range(KT):
                    if k == 2:
                        split_lo(BASE[s] + 4)
                    q = 16 * s + k
                    dve.wait_ge(sq_ready, q + 1)
                    if k == 0:
                        dve.tensor_copy(acc[:, :], sq[:, 0, :]).then_inc(acc_done, 1)
                    else:
                        dve.wait_ge(acc_done, q)
                        dve.tensor_tensor(acc[:, :], acc[:, :], sq[:, q % 2, :], ALU.add).then_inc(acc_done, 1)
                split_lo(BASE[s] + 5)

            def y_of(s):
                return y_ffn if s >= 0 and STAGES[s] == "ffn" else y_mix

            def stat_ms(n):
                dve.wait_ge(stat_sum, n + 1)
                dve.tensor_scalar(ms[:, 0:TT], ps[:, STAT, 0:TT], EPS, None, ALU.add).then_inc(ms_ready, 1)

            def stat_rcol(n):
                dve.wait_ge(root_ready, n + 1)
                dve.reciprocal(rcol[:, 0:TT], root[:, 0:TT]).then_inc(rcol_ready, 1)
                dve.memset(acc[:, :], 0.0).then_inc(acc_cleared, 1)

            def hidden(e, ub, c, m, i, banks=None):
                n = e + m * i
                gate, up = banks or (2 * (c % 2), 2 * (c % 2) + 1)
                dve.wait_ge(unit_used, ub + 2 * c + 1 + 2 * m * i)
                dve.tensor_tensor(ta[:, :], ps[:, gate, :], rs[:, :], ALU.mult).then_inc(gate_scaled, 1)
                dve.wait_ge(unit_used, ub + 2 * c + 2 + 2 * m * i)
                if e or not isinstance(i, int):
                    dve.wait_ge(hid_lo, n)
                dve.tensor_tensor(tb[:, :], ps[:, up, :], rs[:, :], ALU.mult).then_inc(up_scaled, 1)
                dve.wait_ge(up_scaled, n + 1)
                dve.wait_ge(silu_ready, n + 1)
                dve.tensor_tensor(tb[:, :], tb[:, :], tc[:, :], ALU.mult).then_inc(hid_ready, 1)
                dve.wait_ge(hid_hi, n + 1)
                f = bass.ds(c + m * i, 1)
                dve.tensor_tensor(h_lo[:, f, :].rearrange("p a t -> p (a t)"), tb[:, :],
                                  h_hi[:, f, :].rearrange("p a t -> p (a t)").bitcast(F32),
                                  ALU.subtract).then_inc(hid_lo, 1)

            def ffn(s):
                ub, e0 = BASE[s], FT * FFN_OF[s]
                input_tiles(s)
                input_squares(s)
                split_lo(ub + 6)
                stat_ms(stat_no(s, 0))
                stat_rcol(stat_no(s, 0))
                split_lo(ub + 7)
                dve.wait_ge(rs_ready, s + 1)
                for c in range(4):
                    if c == 3:
                        split_lo(ub + 8)
                        split_lo(ub + 9)
                    hidden(e0 + c, ub, c, 0, 0, FIRST_BANKS[2 * c:2 * c + 2])
                with dve.Fori(2, FT // 2) as i:
                    for j in range(2):
                        split_lo(ub + 2 * j + 2, 4, i)
                        split_lo(ub + 2 * j + 3, 4, i)
                        hidden(e0 + j, ub, j, 2, i)
                vb = ub + 2 * FT
                split_lo(vb + 2, 0, 0, DOWN[2] * P)

                def output_tiles(i, n):
                    for d in range(n):
                        for b in range(3):
                            split_lo(vb + 3 * d + b + 3, 12, i, DOWN[b] * P)
                        add_square(16 * s + 8 + d, 4, i, s)

                with dve.Fori(0, KT // 4 - 1) as i:
                    output_tiles(i, 4)
                output_tiles(KT // 4 - 1, 3)
                if s + 1 < len(STAGES):
                    split_lo(BASE[s + 1])
                tail(s)

            def mlstm(s):
                ub = BASE[s]
                input_tiles(s)
                input_squares(s)
                for u in range(M_UNITS - 2):
                    if u == M_GATE:
                        split_lo(ub + M_GATE + 2)
                        stat_ms(stat_no(s, 0))
                        stat_rcol(stat_no(s, 0))
                        split_lo(ub + M_GATE + 3)
                    if M_GATE < u:
                        split_lo(ub + u + 3)
                    if u == M_GATE:
                        dve.wait_ge(unit_used, ub + M_GATE + 1)
                        dve.wait_ge(rs_ready, 2)
                        dve.tensor_tensor(m_e[0:40, 1, 1, :], ps[0:40, 6, :], rs[0:40, :], ALU.mult).then_inc(gate_z, 1)
                    if u == M_V1:
                        gates()
                    if u == M_V1 + 2:
                        dve.wait_ge(max_hi, 1)
                        dve.tensor_tensor(m_max_lo[:, :], m_max[:, :], m_max_hi[:, :].bitcast(F32),
                                          ALU.subtract).then_inc(max_lo, 1)
                    if M_QK <= u < M_QK + KT:
                        qk_tile(ub, u, u - M_QK)
                    if u == M_V1 + 3:
                        dve.wait_ge(acol_sum, 1)
                        dve.tensor_copy(acol[:, :], ps[:, 6, 0:TT * HEADS]).then_inc(acol_ready, 1)
                    if u == M_O + KT - 1:
                        head_scores(0)
                    if M_O <= u < M_O + KT:
                        c = u - M_O
                        dve.wait_ge(unit_used, ub + u + 1)
                        if c >= 2:
                            dve.wait_ge(o_tanh, c - 1)
                        else:
                            dve.wait_ge(qk_silu, KT)
                        dve.tensor_tensor((ta, tb)[c % 2][:, :], ps[:, o_bank(c), :], rs[:, :],
                                          ALU.mult).then_inc(o_read, 1)
                    if u == M_OUT - 1:
                        heads(s)
                    if M_OUT <= u:
                        if u - M_OUT < HALVED["mlstm"][0]:
                            add_square(16 * s + 8 + u - M_OUT, 0, 0, s)
                tail(s)

            def gates():
                dve.wait_ge(gate_l, 1)
                run, soft, a, top = (m_e[0:HEADS, 0, j, :] for j in range(4))
                dve.wait_ge(zeroed, 6)
                link(dve.tensor_tensor_scan(run, zeros[:, :], soft, 0.0, ALU.add, ALU.add))
                link(dve.scalar_tensor_tensor(out=a, in0=tc[0:HEADS, :], scalar=CAP, in1=run, op0=ALU.mult,
                                              op1=ALU.add))
                link(dve.tensor_tensor_scan(top, zeros[:, :], a, 0.0, ALU.add, ALU.max))
                dve.wait_ge(region_zero, 3)
                dve.tensor_scalar(m_max[0:HEADS, :], top, -1.0, None, ALU.mult).then_inc(gates_done, 1)
                dve.tensor_tensor(m_e[0:HEADS, 1, 0, :], run, top, ALU.subtract).then_inc(gates_done, 1)

            def qk_tile(ub, u, c):
                dve.wait_ge(unit_used, ub + u + 1)
                if c:
                    dve.wait_ge(conv_ready, c)
                dve.tensor_tensor(u_conv[:, TAPS - 1:], ps[:, c % 2, :], rs[:, :], ALU.mult).then_inc(qk_read, 1)
                dve.wait_ge(qk_read, c + 1)
                buf = (ta, tb)[c % 2][:, :]
                if c >= 2:
                    dve.wait_ge(qk_silu, c - 1)
                w = C_CONVW + c * TAPS
                for j in range(TAPS):
                    if j == 0:
                        ins = dve.tensor_scalar(buf, u_conv[:, 0:T], consts[:, w:w + 1],
                                                consts[:, C_CONVB + c:C_CONVB + c + 1], ALU.mult, ALU.add)
                    else:
                        ins = dve.scalar_tensor_tensor(out=buf, in0=u_conv[:, j:j + T],
                                                       scalar=consts[:, w + j:w + j + 1], in1=buf,
                                                       op0=ALU.mult, op1=ALU.add)
                    if j < TAPS - 1:
                        link(ins)
                    else:
                        ins.then_inc(conv_ready, 1)

            def head_scores(h):
                dve.wait_ge(e_ready, TT * (h + 1))
                diag = m_e[:, h % 2, :, 0:P]
                dve.wait_ge(selected, 2)
                dve.scalar_tensor_tensor(out=diag, in0=diag, scalar=BIG,
                                         in1=causal[:, :].unsqueeze(1).to_broadcast([P, TT, P]),
                                         op0=ALU.min, op1=ALU.mult).then_inc(e_masked, 1)
                dve.wait_ge(e_masked, h + 1)
                dve.wait_ge(s_ready, h + 1)
                if h >= 2:
                    dve.wait_ge(den_ready, h - 1)
                for st in range(TT):
                    bank, at = ((0, 0), (1, 0), (2, 0), (2, 256))[st]
                    dve.scalar_tensor_tensor(out=m_sc[:, h % 2, OFF[st]:OFF[st] + CAUSAL[st]],
                                             in0=ps[:, bank, at:at + CAUSAL[st]], scalar=DQK ** -0.5,
                                             in1=m_e[:, h % 2, st, 0:CAUSAL[st]], op0=ALU.mult,
                                             op1=ALU.mult).then_inc(sc_done, 1)
                tot = (ta, tb)[h % 2]
                dve.wait_ge(o_tanh, KT - 1 + h % 2)
                for st in range(1, TT):
                    cols = slice(P * st, T)
                    dve.wait_ge(sc_done, TT * h + st + 1)
                    if st > 1:
                        dve.wait_ge(tot_done, (TT - 1) * h + st - 1)
                    one = m_sc[:, h % 2, P * st:T] if st == 1 else tot[:, cols]
                    dve.tensor_tensor(tot[:, cols], one, m_sc[:, h % 2, OFF[st]:OFF[st] + CAUSAL[st]],
                                      ALU.add).then_inc(tot_done, 1)

            def heads(s):
                for h in range(1, HEADS + 1):
                    if h < HEADS:
                        head_scores(h)
                    if h == 5:
                        heads_mean(0)
                    if h == 6:
                        heads_rescale(0)
                    if h >= 1:
                        g = h - 1
                        dve.wait_ge(hsq_ready, g + 1)
                        dve.scalar_tensor_tensor(out=m_o[:, g, :], in0=m_o[:, g, :], scalar=1.0,
                                                 in1=ps[:, 5 + g % 2, :], op0=ALU.add,
                                                 op1=ALU.mult).then_inc(og_ready, 1)
                for h in range(HEADS):
                    dve.wait_ge(head_bcast, h + 1)
                    dve.wait_ge(og_ready, h + 1)
                    dve.tensor_tensor(m_o[:, h, :], m_o[:, h, :], ps[:, 3 + h % 2, :],
                                      ALU.mult).then_inc(og_scaled, 1)
                    dve.wait_ge(op_hi, KT * OUT_SET[s] + h + 1)
                    dve.wait_ge(og_scaled, h + 1)
                    col = C_HEADG + h
                    dve.scalar_tensor_tensor(out=x_lo[:, h, :], in0=m_o[:, h, :],
                                             scalar=half_gain[:, col:col + 1], in1=x_hi[:, h, :].bitcast(F32),
                                             op0=ALU.mult, op1=ALU.subtract).then_inc(op_lo, 1)
                    if h == 0:
                        heads_mean(1)
                    if h == 1:
                        heads_rescale(1)

            def heads_mean(g):
                cols = slice(TT * 4 * g, TT * 4 * (g + 1))
                dve.wait_ge(stat_heads, 4 * (g + 1))
                dve.wait_ge(den_ready, 5 + 3 * g)
                dve.wait_ge(floor_ready, 1)
                den_sum = ps[:, STAT, cols]
                link(dve.scalar_tensor_tensor(out=dmag[:, cols], in0=den_sum, scalar=-1.0,
                                              in1=floor[:, 4 * g:4 * g + 4, :].rearrange("p h t -> p (h t)"),
                                              op0=ALU.mult, op1=ALU.max))
                link(dve.tensor_tensor(dmag[:, cols], dmag[:, cols], den_sum, ALU.max))
                link(dve.reciprocal(dinv[:, cols], dmag[:, cols]))
                dve.tensor_tensor(dneg[:, cols], dinv[:, cols], ps[:, STAT, 256 + cols.start:256 + cols.stop],
                                  ALU.mult).then_inc(heads_read, 1)
                dve.wait_ge(heads_read, g + 1)
                link(dve.tensor_tensor(dneg[:, cols], dneg[:, cols], dinv[:, cols], ALU.mult))
                dve.tensor_scalar(ms[:, cols], dneg[:, cols], EPS, None, ALU.add).then_inc(heads_ms, 1)

            def heads_rescale(g):
                cols = slice(TT * 4 * g, TT * 4 * (g + 1))
                dve.wait_ge(heads_root, g + 1)
                link(dve.reciprocal(dneg[:, cols], root[:, cols]))
                dve.tensor_tensor(rcol[:, cols], dneg[:, cols], dinv[:, cols], ALU.mult).then_inc(heads_rcol, 1)

            def window(s):
                ub = BASE[s]
                input_tiles(s)
                input_squares(s)
                split_lo(ub + 6)
                stat_ms(stat_no(s, 0))
                stat_rcol(stat_no(s, 0))
                split_lo(ub + 7)
                dve.wait_ge(rs_ready, s + 1)
                for u in range(W_UNITS - 2):
                    if u > 4:
                        split_lo(ub + u + 3)
                    if u < W_V:
                        dve.wait_ge(unit_used, ub + u + 1)
                    if u < W_K:
                        dve.tensor_tensor(b_q[:, u // 2, :, u % 2, :],
                                          ps[:, W_BANKS[u], :].rearrange("p (n t) -> p n t", n=NCH),
                                          rs[:, :].rearrange("p (n t) -> p n t", n=NCH),
                                          ALU.mult).then_inc(b_read, 1)
                    if u == W_K:
                        dve.wait_ge(region_zero, 3 + 2 * KV)
                        for g in range(KV):
                            for par in range(2):
                                src = slice(g * HD, g * HD + HD)
                                dve.scalar_tensor_tensor(out=b_k[g][par][par * HD:par * HD + HD, :],
                                                         in0=ps[src, W_BANKS[u], :], scalar=-HD ** -0.5,
                                                         in1=rs[src, :], op0=ALU.mult,
                                                         op1=ALU.mult).then_inc(b_read, 1)
                    if u == W_V:
                        chunk_max(0)
                        dve.wait_ge(unit_used, ub + u + 1)
                        dve.tensor_tensor(ta[:, :], ps[:, W_BANKS[u], :], rs[:, :], ALU.mult).then_inc(bv_ready, 1)
                        chunk_max(1)
                        for n in range(NCH + 1):
                            if n < NCH - 1:
                                chunk_divide(n)
                            if n + 2 < NCH:
                                chunk_max(n + 2)
                            elif n == NCH - 2:
                                chunk_divide(NCH - 1)
                            if n < NCH:
                                chunk_turn(n)
                            if n >= 1:
                                chunk_rest(s, n - 1)
                    if W_OUT <= u:
                        if u - W_OUT < HALVED["window"][0]:
                            add_square(16 * s + 8 + u - W_OUT, 0, 0, s)
                tail(s)

            def chunk_max(n):
                b = n % 2
                keys = slice(0, CHUNK if n == 0 else P)
                sink = consts[:, C_SINK:C_SINK + 8]
                dve.wait_ge(bs_ready, n + 1)
                scores = ps[:, 2 * b:2 * b + 2, :].rearrange("p a (c k) -> p (a c) k", c=4)[:, :, keys]
                link(dve.tensor_reduce(low[:, b, :], scores, AX_X, ALU.min))
                dve.scalar_tensor_tensor(out=nmx[:, b, :], in0=sink, scalar=-1.0, in1=low[:, b, :],
                                         op0=ALU.mult, op1=ALU.min).then_inc(nmx_ready, 1)
                dve.wait_ge(nmx_ready, n + 1)
                dve.tensor_tensor(smx[:, b, :], sink, nmx[:, b, :], ALU.add).then_inc(smx_ready, 1)

            def chunk_divide(n):
                b = n % 2
                nk = CHUNK if n == 0 else P
                keys = slice(0, nk)
                dve.wait_ge(p_exp, 9 * (n + 1))
                link(dve.tensor_tensor(den[:, b, :], sm[:, b, :], esk[:, b, :], ALU.add))
                link(dve.reciprocal(rden[:, b, :], den[:, b, :]))
                p = b_p[:, b, :, keys]
                dve.tensor_tensor(p, p, rden[:, b, :].unsqueeze(2).to_broadcast([P, 8, nk]),
                                  ALU.mult).then_inc(p_ready, 1)

            def chunk_turn(n):
                rows = slice(0, CHUNK if n == 0 else P)
                dve.wait_ge(pt_ready, n + 1)
                if n >= 2:
                    dve.wait_ge(po_ready, n - 1)
                dve.tensor_copy(b_pt[rows, n % 2, 4:8, :],
                                ps[rows, 5, :].rearrange("p (a b) -> p a b", a=4)).then_inc(pt_dve, 1)

            def chunk_rest(s, n):
                dve.wait_ge(op_hi, KT * OUT_SET[s] + n + 1)
                toks = slice(n * CHUNK, (n + 1) * CHUNK)
                dve.tensor_tensor(x_lo[:, :, toks], ps[:, 6 + n % 2, :].rearrange("p (a b) -> p a b", a=8),
                                  x_hi[:, :, toks].bitcast(F32), ALU.subtract).then_inc(op_lo, 1)

            dve.wait_ge(consts_landed, 16)
            dve.tensor_scalar(half_gain[:, :], consts[:, 0:C_CONVW], 0.5, None, ALU.mult).then_inc(scaled_consts, 1)
            dve.tensor_scalar(gate_b15[:, :], consts[:, C_GATEB:C_GATEB + 1], 1.0 / CAP, None,
                              ALU.mult).then_inc(scaled_consts, 1)
            for s, kind in enumerate(STAGES):
                {"ffn": ffn, "mlstm": mlstm, "window": window}[kind](s)
            residual(len(STAGES) - 1, 1)

        @block.tensor
        def _(pe):
            def three(dst, w, cols, mv, toks, start, stop, swap=False):
                for n, (a, b) in enumerate(((0, 0), (1, 0), (0, 1))):
                    lhs, rhs = w[a][cols], mv[b][toks]
                    if swap:
                        lhs, rhs = rhs, lhs
                    ins = pe.matmul(dst, lhs, rhs, start=start and n == 0, stop=stop and n == 2)
                return ins

            W, X, H = (w_hi, w_lo), (x_hi, x_lo), (h_hi, h_lo)
            ALL = slice(None)

            def block_cols(c, b, n=P):
                return (ALL, c % RING, slice(b * P, b * P + n))

            def unit(c, m, i, bank, midway=None, when=KT // 2):
                pe.wait_ge(lo_split, c + 1 + m * i)
                for k in range(KT):
                    if midway and k == when:
                        midway()
                    ins = three(ps[:, bank, :], W, block_cols(c, k), X, (ALL, k), k == 0, k == KT - 1)
                ins.then_inc(unit_used, 1)

            def three_units(c, tiles_before, between=None, cols=slice(0, T)):
                pe.wait_ge(lo_split, c + 3)
                for k in range(KT):
                    pe.wait_ge(op_lo, tiles_before + k + 1)
                    for j in range(3):
                        ins = three(ps[:, j, cols], W, block_cols(c + j, k), X, (ALL, k, cols), k == 0, k == KT - 1)
                        if k == KT - 1:
                            ins.then_inc(unit_used, 1)
                    if between:
                        between(k)

            def sum_squares(q):
                pe.wait_ge(acc_done, q)
                for t in range(TT):
                    ins = pe.matmul(ps[:, STAT, t:t + P], acc[:, t * P:(t + 1) * P], inv_d[:, :],
                                    start=True, stop=True)
                ins.then_inc(stat_sum, 1)

            def spread(bank, at, done):
                for t in range(TT):
                    ins = pe.matmul(ps[:, bank, t * P:(t + 1) * P], rcol[:, at + t:at + t + 1].to_broadcast([P, P]),
                                    ident[:, :], start=True, stop=True)
                ins.then_inc(done, 1)

            def spread_pre(s):
                pe.wait_ge(rcol_ready, stat_no(s, 0) + 1)
                spread(STAT, 0, bcast_ready)

            def spread_head(h):
                pe.wait_ge(heads_rcol, h // 4 + 1)
                if h < 2:
                    pe.wait_ge(e_ready, TT * (7 + h))
                else:
                    pe.wait_ge(og_scaled, h - 1)
                spread(3 + h % 2, TT * h, head_bcast)

            def sum_half(s, h):
                if h:
                    pe.wait_ge(acc_done, 16 * s + 16)
                else:
                    pe.wait_ge(first_acc, first_tiles(s + 1))
                for t in (2 * h, 2 * h + 1):
                    ins = pe.matmul(ps[:, (STAT, STAT_B)[h], t:t + P], acc[:, t * P:(t + 1) * P], inv_d[:, :],
                                    start=True, stop=True)
                ins.then_inc((first_sum, stat_sum)[h], 1)

            def spread_half(s, h):
                if h:
                    pe.wait_ge(rcol_ready, stat_no(s, 1) + 1)
                else:
                    pe.wait_ge(first_rcol, s + 1)
                for t in (2 * h, 2 * h + 1):
                    ins = pe.matmul(ps[:, (STAT, STAT_B)[h], t * P:(t + 1) * P],
                                    rcol[:, t:t + 1].to_broadcast([P, P]), ident[:, :], start=True, stop=True)
                ins.then_inc((first_bcast, bcast_ready)[h], 1)

            def first_norm(s, step):
                if step == 3:
                    sum_half(s, 0)
                if step == 6:
                    spread_half(s, 0)

            def second_norm(s, h, k):
                if s and h == 0 and k == 2:
                    sum_half(s - 1, 1)
                if s and h == 0 and k == 6:
                    spread_half(s - 1, 1)

            def pair(ub, e0, c, m, i, j):
                pe.wait_ge(up_scaled, e0 + c + j - 1 + m * i)
                for half in range(2):
                    unit(ub + 2 * (c + j) + half, 2 * m, i, 2 * (j % 2) + half)

            def begin(s, banks):
                ub = BASE[s]
                lag = (0, 0, 2, 4) if s else (0, 0, 0, KT)
                for h in range(2) if s else (0,):
                    cols = HALF[h] if s else slice(0, T)
                    for k in range(KT + lag[3]):
                        second_norm(s, h, k)
                        if k < KT and s:
                            pe.wait_ge(in_lo[h], KT * (s - 1) + k + 1)
                        elif k < KT:
                            if k < KT - 3:
                                pe.wait_ge(start_lo, k + 1)
                            else:
                                pe.wait_ge(lo_split, k - (KT - 3) + 1)
                            pe.wait_ge(op_lo, k + 1)
                        for j in range(4):
                            at = k - lag[j]
                            if not 0 <= at < KT:
                                continue
                            if at == 0 and (s or j == 3):
                                pe.wait_ge(lo_split, ub + j + 1)
                            ins = three(ps[:, banks[j], cols], W, block_cols(ub + j, at), X, (ALL, at, cols),
                                        at == 0, at == KT - 1)
                            if at == KT - 1 and (h or s == 0):
                                ins.then_inc(unit_used, 1)

            def prenorm(s, c, banks):
                unit(BASE[s] + c, 0, 0, banks[0])
                sum_squares(16 * s + 8)
                unit(BASE[s] + c + 1, 0, 0, banks[1], lambda: spread_pre(s))

            def ffn(s):
                ub, e0 = BASE[s], FT * FFN_OF[s]
                if e0:
                    pe.wait_ge(up_scaled, e0)
                begin(s, FIRST_BANKS)
                prenorm(s, 4, (0, 1))
                unit(ub + 6, 0, 0, 2)
                pe.wait_ge(up_scaled, e0 + 2)
                unit(ub + 7, 0, 0, 3)
                with pe.Fori(2, FT // 2) as i:
                    for j in range(2):
                        pair(ub, e0, 0, 2, i, j)
                vb = ub + 2 * FT

                def down_tile(d, i, bank, cols, half=None):
                    at = 0
                    for b, blocks in enumerate(DOWN):
                        c = vb + 3 * d + b
                        pe.wait_ge(lo_split, c + 1 + 12 * i)
                        if b == 0 and d != 1 and not half:
                            pe.wait_ge(sq_ready, 16 * s + 8 + d - 1 + 4 * i)
                        for f in range(at, at + blocks):
                            if f in (FT - 2, FT - 1) and d == 0:
                                pe.wait_ge(hid_lo, e0 + f + 1)
                            elif f == 0 and d == 0:
                                pe.wait_ge(hid_lo, e0 + FT - 2)
                            if half:
                                first_norm(s, f)
                            ins = three(ps[:, bank, cols], W, block_cols(c, f - at), H, (ALL, f, cols),
                                        f == 0, f == FT - 1)
                        at += blocks
                        if half != 0:
                            ins.then_inc(unit_used, 1)
                        elif b == len(DOWN) - 1:
                            ins.then_inc(first_done, 1)

                with pe.Fori(0, KT // 4 - 1) as i:
                    for d in range(4):
                        down_tile(d, i, DOWN_BANK[d], ALL)
                for d in range(3):
                    down_tile(d, KT // 4 - 1, DOWN_BANK[d], ALL)
                down_tile(3, KT // 4 - 1, DOWN_BANK[3], HALF[0], 0)
                down_tile(3, KT // 4 - 1, SECOND_BANK[0], HALF[1], 1)
                if s + 1 == len(STAGES):
                    sum_half(s, 1)
                    spread_half(s, 1)

            def v_unit(ub, first, u, h=None):
                c = ub + first + u
                pe.wait_ge(lo_split, c + 1)
                for kk in range(2):
                    k = 2 * u + kk
                    if first == M_V0:
                        second_norm(1, h, k)
                        pe.wait_ge(in_lo[h], k + 1)
                    for tt in range(TT) if h is None else (2 * h, 2 * h + 1):
                        ins = three(ps[:, V_BANKS[tt], :], W, (ALL, c % RING, slice(kk * T, kk * T + T)), X,
                                    (ALL, k, slice(tt * P, tt * P + P)), k == 0, k == KT - 1, swap=True)
                if h != 0:
                    ins.then_inc(unit_used, 1)

            def mlstm(s):
                ub = BASE[s]
                pe.wait_ge(up_scaled, FT)
                for h in range(2):
                    for u in range(4):
                        v_unit(ub, M_V0, u, h)
                prenorm(s, M_GATE, (6, 0))
                for c in range(1, KT):
                    if c >= 2:
                        pe.wait_ge(qk_read, c - 1)
                    unit(ub + M_QK + c, 0, 0, c % 2)
                pe.wait_ge(v_kept, TT)
                for u in range(4):
                    v_unit(ub, M_V1, u)
                pe.wait_ge(gates_done, 2)
                for j, rows in enumerate((m_e[0:HEADS, 0, 2, :], m_e[0:HEADS, 1, 0, :])):
                    for st in range(TT):
                        at = (TT * j + st) * HEADS
                        ins = pe.matmul(ps[:, 6, at:at + HEADS], rows[:, st * P:(st + 1) * P],
                                        ident[0:HEADS, 0:HEADS], start=True, stop=True)
                ins.then_inc(acol_sum, 1)
                for c in range(KT):
                    if c >= 2:
                        pe.wait_ge(o_read, c - 1)
                    else:
                        pe.wait_ge(qk_read, KT - 1 + c)
                    if c == KT - 1:
                        pe.wait_ge(region_zero, 3)
                        head_scores(0)
                    if c == 2:
                        pe.wait_ge(v_kept, 2 * TT)
                    unit(ub + M_O + c, 0, 0, o_bank(c))
                heads(s)

            def head_scores(h):
                if h == 0:
                    pe.wait_ge(v_kept, 2 * TT)
                if h == 1:
                    pe.wait_ge(o_read, KT - 1)
                if h >= 2:
                    pe.wait_ge(e_ready, TT * (h - 1))
                pe.wait_ge(ident_ready, 1)
                pe.wait_ge(max_lo, 1)
                row = ident_hi[:, h:h + 1].to_broadcast([P, P])
                pe.matmul(ps[:, 3 + h % 2, :], row, m_max_hi[:, :], start=True, stop=False)
                pe.matmul(ps[:, 3 + h % 2, :], row, m_max_lo[:, :], start=False, stop=True).then_inc(max_ready, 1)
                if h:
                    pe.wait_ge(sc_done, TT * h)
                j, par = divmod(h, 2)
                for st in range(TT):
                    bank, at = ((0, 0), (1, 0), (2, 0), (2, 256))[st]
                    ins = pe.matmul(ps[:, bank, at:at + CAUSAL[st]], m_k[par][:, j, st * P:(st + 1) * P],
                                    m_q[:, j, st * P:T], start=True, stop=True)
                ins.then_inc(s_ready, 1)

            def heads(s):
                for h in range(HEADS + 1):
                    if h + 1 < HEADS:
                        head_scores(h + 1)
                    if h < HEADS:
                        pe.wait_ge(sc_done, TT * (h + 1))
                        if h == 0:
                            pe.wait_ge(o_read, KT)
                        elif h == 1:
                            pe.wait_ge(floor_ready, 1)
                        else:
                            pe.wait_ge(og_ready, h - 1)
                        for st in range(TT):
                            ins = pe.matmul(ps[:, 5 + h % 2, P * st:T], m_v[:, st, h * P:(h + 1) * P],
                                            m_sc[:, h % 2, OFF[st]:OFF[st] + CAUSAL[st]],
                                            start=st == 0, stop=st == TT - 1)
                        ins.then_inc(num_ready, 1)
                    if h >= 1:
                        g = h - 1
                        pe.wait_ge(hsq_ready, g + 1)
                        if g == 4:
                            pe.wait_ge(heads_read, 1)
                        for t in range(TT):
                            at = 256 + TT * g + t
                            ins = pe.matmul(ps[:, STAT, at:at + P], sq[:, h % 2, t * P:(t + 1) * P],
                                            inv_dv[:, :], start=True, stop=True)
                        ins.then_inc(stat_heads, 1)
                    if h < HEADS:
                        pe.wait_ge(tot_done, (TT - 1) * (h + 1))
                        for t in range(TT):
                            at = TT * h + t
                            tot = m_sc[:, h % 2, 0:P] if t == 0 else (ta, tb)[h % 2][:, t * P:(t + 1) * P]
                            ins = pe.matmul(ps[:, STAT, at:at + P], tot, ones[:, :], start=True, stop=True)
                        ins.then_inc(den_ready, 1)
                        if h == HEADS - 1:
                            spread_head(0)
                            spread_head(1)

                def next_head(k):
                    if k + 2 < HEADS:
                        spread_head(k + 2)

                three_units(BASE[s] + M_OUT, KT * OUT_SET[s], next_head)
                out_product(s, M_OUT)

            def out_product(s, first):
                ub = BASE[s] + first
                here = HALVED[STAGES[s]]
                for d in range(3, here[0]):
                    unit(ub + d, 0, 0, out_bank(s, d))
                for h in range(2):
                    for n, d in enumerate(here):
                        pe.wait_ge(lo_split, ub + d + 1)
                        if h == 0 and d >= 6:
                            pe.wait_ge(sq_ready, 16 * s + 8 + d - 2)
                        for k in range(KT):
                            if h:
                                first_norm(s, KT * n + k)
                            ins = three(ps[:, SECOND_BANK[n] if h else out_bank(s, d), HALF[h]], W,
                                        block_cols(ub + d, k), X, (ALL, k, HALF[h]), k == 0, k == KT - 1)
                        ins.then_inc(unit_used if h else first_done, 1)

            def window(s):
                ub = BASE[s]
                pe.wait_ge(up_scaled, FT * 3)
                begin(s, FIRST_BANKS)
                prenorm(s, 4, (0, 1))
                for u in range(6, W_V):
                    if u >= 7:
                        pe.wait_ge(b_read, u - 6)
                    unit(ub + u, 0, 0, W_BANKS[u])

                def first_scores():
                    pe.wait_ge(b_read, 8 + 4)
                    for n in range(2):
                        chunk_scores(n)

                pe.wait_ge(b_read, W_V - 6)
                unit(ub + W_V, 0, 0, W_BANKS[W_V], first_scores, 6)
                pe.wait_ge(bv_ready, 1)
                for n in range(NCH):
                    nk = CHUNK if n == 0 else P
                    lo = max(n - 1, 0) * CHUNK
                    pe.transpose(ps[0:nk, 4 + n // 4, (n % 4) * P:(n % 4) * P + P], ta[:, lo:lo + nk],
                                 ident[:, :]).then_inc(bw_ready, 1)
                chunk_scores(2)
                blocks = [(j, k) for j in range(3) for k in range(KT)]

                def early(first, last):
                    for j, k in blocks[first:last]:
                        if k == 0:
                            pe.wait_ge(lo_split, ub + W_OUT + j + 1)
                            pe.wait_ge(op_lo, KT * OUT_SET[s] + NCH // 2)
                            pe.wait_ge(p_exp, 9 * (NCH - 1 if j < 2 else NCH))
                        three(ps[:, j, HALF[0]], W, block_cols(ub + W_OUT + j, k), X, (ALL, k, HALF[0]),
                              k == 0, k == KT - 1)

                for n in range(NCH):
                    chunk_turn(n)
                    if n + 3 < NCH:
                        chunk_scores(n + 3)
                    if n == NCH - 2:
                        early(4, 8)
                    if n == NCH - 1:
                        early(13, 16)
                    chunk_values(n)
                    if n == NCH - 3:
                        early(0, 4)
                    if n == NCH - 2:
                        early(8, 13)
                early(16, 24)
                pe.wait_ge(op_lo, KT * (OUT_SET[s] + 1))
                three_units(ub + W_OUT, KT * OUT_SET[s], None, HALF[1])
                out_product(s, W_OUT)

            def chunk_scores(n):
                nk = CHUNK if n == 0 else P
                lo = max(n - 1, 0) * CHUNK
                if n >= 2:
                    pe.wait_ge(p_exp, 9 * (n - 1))
                for i in range(8):
                    g, par, jp = i // 4, i // 2 % 2, i % 2
                    j = 4 * g + 2 * jp
                    at = (i % 4) * P
                    ins = pe.matmul(ps[:, 2 * (n % 2) + i // 4, at:at + nk],
                                    b_q[:, j // 2, n, :, :].rearrange("p a t -> p (a t)"), b_k[g][par][:, lo:lo + nk],
                                    start=True, stop=True)
                ins.then_inc(bs_ready, 1)

            def chunk_turn(n):
                nk = CHUNK if n == 0 else P
                pe.wait_ge(p_ready, n + 1)
                if n == 0:
                    pe.wait_ge(bw_kept, 3)
                else:
                    pe.wait_ge(pt_act, n)
                    pe.wait_ge(pt_dve, n)
                for i in range(8):
                    ins = pe.transpose(ps[0:nk, 4 + i // 4, (i % 4) * P:(i % 4) * P + P],
                                       b_p[:, n % 2, i, 0:nk], ident[:, :])
                ins.then_inc(pt_ready, 1)

            def chunk_values(n):
                nk = CHUNK if n == 0 else P
                pe.wait_ge(pt_act, n + 1)
                pe.wait_ge(pt_dve, n + 1)
                if n >= 2:
                    pe.wait_ge(op_lo, KT * OUT_SET[4] + n - 1)
                for g in range(KV):
                    for par in range(2):
                        i = 4 * g + 2 * par
                        ins = pe.matmul(ps[par * HD:par * HD + HD, 6 + n % 2, g * 256:(g + 1) * 256],
                                        b_v[0:nk, n, g * HD:(g + 1) * HD], b_pt[0:nk, n % 2, i:i + 2, :],
                                        start=True, stop=True)
                ins.then_inc(po_ready, 1)

            pe.wait_ge(selected, 1)
            pe.wait_ge(zeroed, 6)
            for s, kind in enumerate(STAGES):
                {"ffn": ffn, "mlstm": mlstm, "window": window}[kind](s)


def stat_no(s, post):
    return 2 * s + post


def first_tiles(s):
    return sum(len(HALVED[k]) for k in STAGES[:s])


def used_out(s, d):
    first = {1: M_OUT, 4: W_OUT}[s]
    return BASE[s] + first + d + 1


def tiles(np, w):
    k, n = w.shape
    return np.ascontiguousarray(
        w.reshape(k // P, P, n // P, P).transpose(2, 1, 0, 3).reshape(n // P, P, k))


def column_tiles(np, v):
    return v.reshape(-1, P).T


def kernel(x, norm_g, ffn_w_gate, ffn_w_up, ffn_w_down, a_w_in, a_conv_w, a_conv_b, a_gate_b, a_head_g,
           a_w_out, b_w_in, b_sinks, b_w_out, c_w_group, c_scale):
    import numpy as np
    import concourse.bacc as bacc
    from concourse.bass_utils import run_bass_kernel_spmd

    f32 = np.float32
    a = {k: np.asarray(v) for k, v in dict(
        x=x, g=norm_g, wg=ffn_w_gate, wu=ffn_w_up, wd=ffn_w_down, aw=a_w_in, cw=a_conv_w, cb=a_conv_b,
        gb=a_gate_b, hg=a_head_g, ao=a_w_out, bw=b_w_in, bs=b_sinks, bo=b_w_out).items()}
    x_t = np.ascontiguousarray(a["x"][0].T.reshape(KT, P, T).transpose(1, 0, 2))
    gate_up = np.stack([np.stack([tiles(np, a["wg"][l, j]), tiles(np, a["wu"][l, j])], 1).reshape(2 * FT, P, UNIT)
                        for l in range(DEPTH) for j in range(2)])
    down = np.stack([tiles(np, a["wd"][l, j]) for l in range(DEPTH) for j in range(2)])
    aw = a["aw"][0]
    qk, v, o, gate = aw[:, 0:D], aw[:, D:2 * D], aw[:, 2 * D:3 * D], aw[:, 3 * D:]
    gates = np.zeros((D, P), f32)
    gates[:, 0:HEADS] = gate[:, 0:HEADS]
    gates[:, 32:32 + HEADS] = gate[:, HEADS:]
    vt = v.reshape(KT // 2, 2, P, 2, T).transpose(3, 0, 2, 1, 4).reshape(KT, P, UNIT)
    mlstm_w = np.concatenate([vt[0:4], tiles(np, gates), tiles(np, qk), vt[4:8], tiles(np, o),
                              tiles(np, a["ao"][0])])
    window_w = np.concatenate([tiles(np, a["bw"][0]), tiles(np, a["bo"][0])])
    gate_b = np.zeros((P, 1), f32)
    gate_b[0:HEADS, 0] = a["gb"][0, 0:HEADS]
    gate_b[32:32 + HEADS, 0] = a["gb"][0, HEADS:]
    conv_w = a["cw"][0].T.reshape(KT, P, TAPS).transpose(1, 0, 2).reshape(P, KT * TAPS)
    sink = a["bs"][0].reshape(KV, 2, 2, 2).transpose(2, 0, 3, 1).reshape(2, 8)
    consts = np.ascontiguousarray(np.concatenate(
        [column_tiles(np, a["g"].reshape(-1)), column_tiles(np, a["hg"][0]), conv_w, column_tiles(np, a["cb"][0]),
         gate_b, np.repeat(sink, HD, axis=0)], axis=1))

    nc = bacc.Bacc("TRN2", target_bir_lowering=False, num_devices=1)
    arrays, args = {}, []
    for name, arr in (("x_t", x_t), ("consts_in", consts), ("gate_up", gate_up), ("down", down),
                      ("mlstm_w", mlstm_w), ("window_w", window_w)):
        arrays[name] = np.ascontiguousarray(arr)
        args.append(nc.dram_tensor(name, arr.shape, mybir.dt.from_np(arr.dtype), kind="ExternalInput").ap())
    args.append(nc.dram_tensor("out_t", (P, KT, T), F32, kind="ExternalOutput").ap())
    build(nc, *args)
    r = run_bass_kernel_spmd(nc, [arrays], core_ids=[0])
    out = r.results[0]["out_t"]
    return np.ascontiguousarray(out.transpose(2, 1, 0).reshape(1, T, D))
```
